# Optimizing a Trainium2 kernel written in Bass

```python
import jax
import jax.numpy as jnp
from jax import lax
import numpy as np
import math
import jax, jax.numpy as jnp

D_MODEL = 2048
BATCH = 1
SEQ = 256
DEPTH = 1

NSA_HEADS = 16
NSA_KV_GROUPS = 4
HEADS_PER_GROUP = NSA_HEADS // NSA_KV_GROUPS
HEAD_DIM = 128
NSA_WIDTH = NSA_HEADS * HEAD_DIM
KV_WIDTH = NSA_KV_GROUPS * HEAD_DIM
CMP_LEN = 32
CMP_STRIDE = 16
SLC_LEN = 64
SLC_TOP_N = 16
SLC_LOCAL = 2
FORCE_BONUS = 1e4
WINDOW = 512
WIN_Q_BLOCK = 128
SLC_Q_BLOCK = 32

LRU_WIDTH = 2048
LRU_BLOCKS = 16
LRU_BLOCK_DIM = LRU_WIDTH // LRU_BLOCKS
LRU_C = 8.0
LRU_CONV = 4

D_FF = 3 * D_MODEL
FFN_CONV = 3

IN_WIDTH = NSA_WIDTH + 6 * KV_WIDTH + 3 * NSA_HEADS + 2 * LRU_WIDTH + 2 * D_MODEL
NORM_EPS = 1e-6


def rmsnorm(x, g):
    x32 = x.astype(jnp.float32)
    inv = lax.rsqrt(jnp.mean(x32 * x32, axis=-1, keepdims=True) + NORM_EPS)
    return (x32 * inv).astype(x.dtype) * g

def causal_dwconv(x, w, b):
    k = w.shape[0]
    t = x.shape[1]
    xp = jnp.pad(x, ((0, 0), (k - 1, 0), (0, 0)))
    out = b
    for j in range(k):
        out = out + xp[:, j:j + t] * w[j]
    return out

def masked_softmax(s, mask):
    s = jnp.where(mask, s.astype(jnp.float32), -jnp.inf)
    m = jnp.max(s, axis=-1, keepdims=True)
    m = jnp.where(jnp.isfinite(m), m, 0.0)
    p = jnp.exp(s - m)
    return p / jnp.maximum(jnp.sum(p, axis=-1, keepdims=True), 1e-30)

def _split_points():
    sizes = (NSA_WIDTH,) + (KV_WIDTH,) * 6 + (3 * NSA_HEADS, LRU_WIDTH, LRU_WIDTH, D_MODEL, D_MODEL)
    return [int(v) for v in np.cumsum(sizes)[:-1]]

def compress_blocks(kv, pos, w1, w2):
    t = kv.shape[1]
    n_cmp = (t - CMP_LEN) // CMP_STRIDE + 1
    idx = jnp.arange(n_cmp)[:, None] * CMP_STRIDE + jnp.arange(CMP_LEN)[None, :]
    blocks = kv[:, idx] + pos[None, None, :, None, :]
    hid = jax.nn.gelu(jnp.einsum('bnlgd,lde->bnge', blocks, w1))
    return jnp.einsum('bnge,ef->bngf', hid, w2)

def selected_attention(q, k, v, sel):
    bn, t, g, hg, hd = q.shape
    n_slc = t // SLC_LEN
    n_top = sel.shape[-1]
    nc = t // SLC_Q_BLOCK
    kb = k.reshape(bn, n_slc, SLC_LEN, g, hd).transpose(0, 3, 1, 2, 4)
    vb = v.reshape(bn, n_slc, SLC_LEN, g, hd).transpose(0, 3, 1, 2, 4)
    b_ix = jnp.arange(bn)[:, None, None, None]
    g_ix = jnp.arange(g)[None, :, None, None]
    off = jnp.arange(SLC_LEN)
    m_tok = n_top * SLC_LEN

    def chunk(args):
        q_c, sel_c, start = args
        k_g = kb[b_ix, g_ix, sel_c].reshape(bn, g, SLC_Q_BLOCK, m_tok, hd)
        v_g = vb[b_ix, g_ix, sel_c].reshape(bn, g, SLC_Q_BLOCK, m_tok, hd)
        key_pos = (sel_c[..., None] * SLC_LEN + off).reshape(bn, g, SLC_Q_BLOCK, m_tok)
        q_pos = start + jnp.arange(SLC_Q_BLOCK)
        mask = key_pos <= q_pos[None, None, :, None]
        s = jnp.einsum('bqghd,bgqmd->bghqm', q_c, k_g)
        p = masked_softmax(s, mask[:, :, None])
        return jnp.einsum('bghqm,bgqmd->bqghd', p.astype(v_g.dtype), v_g)

    q_chunks = jnp.moveaxis(q.reshape(bn, nc, SLC_Q_BLOCK, g, hg, hd), 1, 0)
    sel_chunks = jnp.moveaxis(sel.reshape(bn, g, nc, SLC_Q_BLOCK, n_top), 2, 0)
    starts = jnp.arange(nc) * SLC_Q_BLOCK
    out = lax.map(chunk, (q_chunks, sel_chunks, starts))
    return jnp.moveaxis(out, 0, 1).reshape(bn, t, g, hg, hd)

def window_attention(q, k, v):
    bn, t, g, hg, hd = q.shape
    nb = t // WIN_Q_BLOCK
    n_prev = WINDOW // WIN_Q_BLOCK

    def band(z):
        zp = jnp.pad(z, ((0, 0), (WINDOW, 0), (0, 0), (0, 0)))
        zb = zp.reshape(bn, nb + n_prev, WIN_Q_BLOCK, g, hd)
        return jnp.concatenate([zb[:, j:j + nb] for j in range(n_prev + 1)], axis=2)

    kb, vb = band(k), band(v)
    qb = q.reshape(bn, nb, WIN_Q_BLOCK, g, hg, hd)
    q_pos = jnp.arange(t).reshape(nb, WIN_Q_BLOCK)
    k_pos = q_pos[:, :1] - WINDOW + jnp.arange((n_prev + 1) * WIN_Q_BLOCK)[None, :]
    diff = q_pos[:, :, None] - k_pos[:, None, :]
    mask = (diff >= 0) & (diff < WINDOW) & (k_pos[:, None, :] >= 0)
    s = jnp.einsum('bnqghd,bnmgd->bnghqm', qb, kb)
    p = masked_softmax(s, mask[None, :, None, None])
    o = jnp.einsum('bnghqm,bnmgd->bnqghd', p.astype(vb.dtype), vb)
    return o.reshape(bn, t, g, hg, hd)

def nsa_attention(q, kc, vc, ks, vs, kw, vw, gates, pos_k, w1_k, w2_k, pos_v, w1_v, w2_v):
    bn, t, _ = q.shape
    g, hg, hd = NSA_KV_GROUPS, HEADS_PER_GROUP, HEAD_DIM
    q = q.reshape(bn, t, g, hg, hd) * (hd ** -0.5)
    kc, vc = kc.reshape(bn, t, g, hd), vc.reshape(bn, t, g, hd)
    ks, vs = ks.reshape(bn, t, g, hd), vs.reshape(bn, t, g, hd)
    kw, vw = kw.reshape(bn, t, g, hd), vw.reshape(bn, t, g, hd)
    t_pos = jnp.arange(t)

    k_cmp = compress_blocks(kc, pos_k, w1_k, w2_k)
    v_cmp = compress_blocks(vc, pos_v, w1_v, w2_v)
    n_cmp = k_cmp.shape[1]
    cmp_start = jnp.arange(n_cmp) * CMP_STRIDE
    cmp_mask = (cmp_start + CMP_LEN - 1)[None, :] <= t_pos[:, None]
    s_cmp = jnp.einsum('btghd,bngd->bghtn', q, k_cmp)
    p_cmp = masked_softmax(s_cmp, cmp_mask)
    o_cmp = jnp.einsum('bghtn,bngd->btghd', p_cmp.astype(v_cmp.dtype), v_cmp)

    n_slc = t // SLC_LEN
    slc_start = jnp.arange(n_slc) * SLC_LEN
    overlap = ((cmp_start[:, None] < slc_start[None, :] + SLC_LEN)
               & (cmp_start[:, None] + CMP_LEN > slc_start[None, :])).astype(jnp.float32)
    imp = jnp.einsum('bghtn,nj->bgtj', p_cmp, overlap)
    blk = jnp.arange(n_slc)[None, :]
    cur = (t_pos // SLC_LEN)[:, None]
    valid = blk <= cur
    forced = (blk == 0) | (valid & (blk > cur - SLC_LOCAL))
    score = jnp.where(forced, imp + FORCE_BONUS, jnp.where(valid, imp, -1.0))
    n_top = min(SLC_TOP_N, n_slc)
    _, sel = lax.top_k(score, n_top)
    o_slc = selected_attention(q, ks, vs, sel)

    o_win = window_attention(q, kw, vw)

    gt = jax.nn.sigmoid(gates.reshape(bn, t, g, hg, 3))
    o = gt[..., 0:1] * o_cmp + gt[..., 1:2] * o_slc + gt[..., 2:3] * o_win
    return o.reshape(bn, t, NSA_WIDTH)

def rg_lru(x, w_a, b_a, w_i, b_i, lam):
    bn, t, w = x.shape
    xb = x.reshape(bn, t, LRU_BLOCKS, LRU_BLOCK_DIM)
    r = jax.nn.sigmoid(jnp.einsum('btnd,nde->btne', xb, w_a).reshape(bn, t, w) + b_a)
    i = jax.nn.sigmoid(jnp.einsum('btnd,nde->btne', xb, w_i).reshape(bn, t, w) + b_i)
    log_a = (LRU_C * r.astype(jnp.float32)) * jax.nn.log_sigmoid(lam.astype(jnp.float32))
    a = jnp.exp(log_a)
    b = jnp.sqrt(-jnp.expm1(2.0 * log_a)) * (i * x).astype(jnp.float32)

    def combine(left, right):
        a1, b1 = left
        a2, b2 = right
        return a1 * a2, a2 * b1 + b2

    _, h = lax.associative_scan(combine, (a, b), axis=1)
    return h.astype(x.dtype)

def token_mixer(h, w_in, pos_k, w1_k, w2_k, pos_v, w1_v, w2_v, conv_w, conv_b,
                w_a, b_a, w_i, b_i, lam, proj_a, proj_b, w_out):
    z = h @ w_in
    q, kc, vc, ks, vs, kw, vw, g_nsa, lx, ly, ga, gb = jnp.split(z, _split_points(), axis=-1)
    o_a = nsa_attention(q, kc, vc, ks, vs, kw, vw, g_nsa, pos_k, w1_k, w2_k, pos_v, w1_v, w2_v)
    u = causal_dwconv(lx, conv_w, conv_b)
    o_b = jax.nn.gelu(ly) * rg_lru(u, w_a, b_a, w_i, b_i, lam)
    merged = jax.nn.sigmoid(ga) * (o_a @ proj_a) + jax.nn.sigmoid(gb) * (o_b @ proj_b)
    return merged @ w_out

def conv_glu_ffn(h, w_up, conv_w, conv_b, w_down):
    gate, val = jnp.split(h @ w_up, 2, axis=-1)
    gate = causal_dwconv(gate, conv_w, conv_b)
    return (jax.nn.gelu(gate) * val) @ w_down

def first_inputs(seed: int = 0) -> dict:
    key = jax.random.key(seed)
    ks = iter(jax.random.split(key, 40))

    def nrm(shape, fan_in, scale=1.0):
        return jax.random.normal(next(ks), shape, jnp.float32) * (scale * fan_in ** -0.5)

    def small(shape, s=0.02):
        return jax.random.normal(next(ks), shape, jnp.float32) * s

    x = jax.random.normal(next(ks), (BATCH, SEQ, D_MODEL), jnp.float32)
    c = jax.random.normal(next(ks), (BATCH, D_MODEL), jnp.float32)
    ada_w = nrm((DEPTH, D_MODEL, 6 * D_MODEL), D_MODEL, 0.5)
    ada_b = small((DEPTH, 6 * D_MODEL))
    norm1_g = 1.0 + small((DEPTH, D_MODEL))
    w_in = nrm((DEPTH, D_MODEL, IN_WIDTH), D_MODEL)
    cmp_pos_k = small((DEPTH, CMP_LEN, HEAD_DIM), 0.1)
    cmp_w1_k = nrm((DEPTH, CMP_LEN, HEAD_DIM, HEAD_DIM), CMP_LEN * HEAD_DIM)
    cmp_w2_k = nrm((DEPTH, HEAD_DIM, HEAD_DIM), HEAD_DIM)
    cmp_pos_v = small((DEPTH, CMP_LEN, HEAD_DIM), 0.1)
    cmp_w1_v = nrm((DEPTH, CMP_LEN, HEAD_DIM, HEAD_DIM), CMP_LEN * HEAD_DIM)
    cmp_w2_v = nrm((DEPTH, HEAD_DIM, HEAD_DIM), HEAD_DIM)
    lru_conv_w = nrm((DEPTH, LRU_CONV, LRU_WIDTH), LRU_CONV)
    lru_conv_b = small((DEPTH, LRU_WIDTH))
    lru_wa = nrm((DEPTH, LRU_BLOCKS, LRU_BLOCK_DIM, LRU_BLOCK_DIM), LRU_BLOCK_DIM)
    lru_ba = small((DEPTH, LRU_WIDTH))
    lru_wi = nrm((DEPTH, LRU_BLOCKS, LRU_BLOCK_DIM, LRU_BLOCK_DIM), LRU_BLOCK_DIM)
    lru_bi = small((DEPTH, LRU_WIDTH))
    u = jax.random.uniform(next(ks), (DEPTH, LRU_WIDTH), jnp.float32)
    rad = jnp.sqrt(u * (0.999 ** 2 - 0.9 ** 2) + 0.9 ** 2)
    lru_lambda = jnp.log(rad) - jnp.log1p(-rad)
    proj_a = nrm((DEPTH, NSA_WIDTH, D_MODEL), NSA_WIDTH)
    proj_b = nrm((DEPTH, LRU_WIDTH, D_MODEL), LRU_WIDTH)
    w_out = nrm((DEPTH, D_MODEL, D_MODEL), D_MODEL)
    norm2_g = 1.0 + small((DEPTH, D_MODEL))
    ffn_up = nrm((DEPTH, D_MODEL, 2 * D_FF), D_MODEL)
    ffn_conv_w = nrm((DEPTH, FFN_CONV, D_FF), FFN_CONV)
    ffn_conv_b = small((DEPTH, D_FF))
    ffn_down = nrm((DEPTH, D_FF, D_MODEL), D_FF)
    final_g = 1.0 + small((D_MODEL,))
    return {"x": x, "c": c, "ada_w": ada_w, "ada_b": ada_b, "norm1_g": norm1_g, "w_in": w_in,
            "cmp_pos_k": cmp_pos_k, "cmp_w1_k": cmp_w1_k, "cmp_w2_k": cmp_w2_k,
            "cmp_pos_v": cmp_pos_v, "cmp_w1_v": cmp_w1_v, "cmp_w2_v": cmp_w2_v,
            "lru_conv_w": lru_conv_w, "lru_conv_b": lru_conv_b, "lru_wa": lru_wa, "lru_ba": lru_ba,
            "lru_wi": lru_wi, "lru_bi": lru_bi, "lru_lambda": lru_lambda,
            "proj_a": proj_a, "proj_b": proj_b, "w_out": w_out, "norm2_g": norm2_g,
            "ffn_up": ffn_up, "ffn_conv_w": ffn_conv_w, "ffn_conv_b": ffn_conv_b, "ffn_down": ffn_down,
            "final_g": final_g}

def first_block(x, c, ada_w, ada_b, norm1_g, w_in, cmp_pos_k, cmp_w1_k, cmp_w2_k, cmp_pos_v, cmp_w1_v,
              cmp_w2_v, lru_conv_w, lru_conv_b, lru_wa, lru_ba, lru_wi, lru_bi, lru_lambda, proj_a, proj_b,
              w_out, norm2_g, ffn_up, ffn_conv_w, ffn_conv_b, ffn_down, final_g):
    c_act = jax.nn.silu(c)
    for l in range(DEPTH):
        mod = (c_act @ ada_w[l] + ada_b[l])[:, None, :]
        sh1, sc1, g1, sh2, sc2, g2 = jnp.split(mod, 6, axis=-1)
        h = rmsnorm(x, norm1_g[l]) * (1.0 + sc1) + sh1
        y = token_mixer(h, w_in[l], cmp_pos_k[l], cmp_w1_k[l], cmp_w2_k[l], cmp_pos_v[l], cmp_w1_v[l],
                        cmp_w2_v[l], lru_conv_w[l], lru_conv_b[l], lru_wa[l], lru_ba[l], lru_wi[l],
                        lru_bi[l], lru_lambda[l], proj_a[l], proj_b[l], w_out[l])
        x = x + g1 * y
        h = rmsnorm(x, norm2_g[l]) * (1.0 + sc2) + sh2
        x = x + g2 * conv_glu_ffn(h, ffn_up[l], ffn_conv_w[l], ffn_conv_b[l], ffn_down[l])
    return rmsnorm(x, final_g)


HEAD_DIM_2 = 64
N_Q_HEADS = D_MODEL // 128
N_KV_HEADS = 4
Q_PER_KV = N_Q_HEADS // N_KV_HEADS
ATTN_W = N_Q_HEADS * HEAD_DIM_2
KV_W = N_KV_HEADS * HEAD_DIM_2
WINDOW_2 = 128
BLOCK = 128
SSM_W = D_MODEL // 2
GROUP = 16
N_GROUPS = SSM_W // GROUP
STATE = 64
IN_SIZES = (ATTN_W, KV_W, KV_W, ATTN_W, SSM_W, SSM_W, D_MODEL, D_MODEL)
IN_W = sum(IN_SIZES)


def rms_norm(x, w):
    xf = x.astype(jnp.float32)
    y = xf * lax.rsqrt(jnp.mean(xf * xf, axis=-1, keepdims=True) + NORM_EPS)
    return (y * w.astype(jnp.float32)).astype(x.dtype)

def sliding_window_attention(q, k, v, sinks):
    b, l = q.shape[0], q.shape[1]
    nb = l // BLOCK
    qb = q.reshape(b, nb, BLOCK, N_KV_HEADS, Q_PER_KV, HEAD_DIM_2)
    kb = k.reshape(b, nb, BLOCK, N_KV_HEADS, HEAD_DIM_2)
    vb = v.reshape(b, nb, BLOCK, N_KV_HEADS, HEAD_DIM_2)
    k_prev = jnp.concatenate([jnp.zeros_like(kb[:, :1]), kb[:, :-1]], axis=1)
    v_prev = jnp.concatenate([jnp.zeros_like(vb[:, :1]), vb[:, :-1]], axis=1)
    kk = jnp.concatenate([k_prev, kb], axis=2)
    vv = jnp.concatenate([v_prev, vb], axis=2)
    scale = 1.0 / math.sqrt(HEAD_DIM_2)
    scores = jnp.einsum('bnqgrd,bnsgd->bngrqs', qb, kk).astype(jnp.float32) * scale
    q_loc = jnp.arange(BLOCK)[:, None] + BLOCK
    k_loc = jnp.arange(2 * BLOCK)[None, :]
    diff = q_loc - k_loc
    k_abs = (jnp.arange(nb)[:, None, None] - 1) * BLOCK + k_loc[None]
    valid = (diff >= 0)[None] & (diff < WINDOW_2)[None] & (k_abs >= 0)
    scores = jnp.where(valid[None, :, None, None], scores, -1e30)
    sink = jnp.broadcast_to(
        sinks.astype(jnp.float32).reshape(1, 1, N_KV_HEADS, Q_PER_KV, 1, 1),
        scores.shape[:-1] + (1,))
    probs = jax.nn.softmax(jnp.concatenate([scores, sink], axis=-1), axis=-1)[..., :-1]
    out = jnp.einsum('bngrqs,bnsgd->bnqgrd', probs.astype(v.dtype), vv)
    return out.reshape(b, l, ATTN_W)

def s5_ssm(u, A_re, A_im, log_dt, B_re, B_im, C_re, C_im, D_skip):
    dt = jnp.exp(log_dt)[:, None]
    mag = jnp.exp(dt * A_re)
    ab_re = mag * jnp.cos(dt * A_im)
    ab_im = mag * jnp.sin(dt * A_im)
    num_re = ab_re - 1.0
    num_im = ab_im
    den = A_re * A_re + A_im * A_im
    cf_re = (num_re * A_re + num_im * A_im) / den
    cf_im = (num_im * A_re - num_re * A_im) / den
    bu_re = jnp.einsum('blgh,gph->blgp', u, B_re)
    bu_im = jnp.einsum('blgh,gph->blgp', u, B_im)
    b_re = cf_re * bu_re - cf_im * bu_im
    b_im = cf_re * bu_im + cf_im * bu_re
    a_re = jnp.broadcast_to(ab_re, b_re.shape)
    a_im = jnp.broadcast_to(ab_im, b_im.shape)

    def combine(e1, e2):
        a1r, a1i, b1r, b1i = e1
        a2r, a2i, b2r, b2i = e2
        return (a2r * a1r - a2i * a1i,
                a2r * a1i + a2i * a1r,
                a2r * b1r - a2i * b1i + b2r,
                a2r * b1i + a2i * b1r + b2i)

    _, _, s_re, s_im = lax.associative_scan(combine, (a_re, a_im, b_re, b_im), axis=1)
    y = (jnp.einsum('blgp,ghp->blgh', s_re, C_re)
         - jnp.einsum('blgp,ghp->blgh', s_im, C_im)
         + D_skip * u)
    return y

def second_inputs(seed: int = 0) -> dict:
    key = jax.random.key(seed)
    ks = jax.random.split(key, 20)
    f32 = jnp.float32
    n = jnp.arange(STATE, dtype=f32)
    x = jax.random.normal(ks[0], (BATCH, SEQ, D_MODEL), f32)
    norm_w = 1.0 + 0.02 * jax.random.normal(ks[1], (D_MODEL,), f32)
    w_in = jax.random.normal(ks[2], (D_MODEL, IN_W), f32) * D_MODEL ** -0.5
    q_norm_w = 1.0 + 0.02 * jax.random.normal(ks[3], (HEAD_DIM_2,), f32)
    k_norm_w = 1.0 + 0.02 * jax.random.normal(ks[4], (HEAD_DIM_2,), f32)
    sinks = jax.random.normal(ks[5], (N_Q_HEADS,), f32)
    w_attn_proj = jax.random.normal(ks[6], (ATTN_W, D_MODEL), f32) * ATTN_W ** -0.5
    A_re = -0.5 + 0.01 * jax.random.normal(ks[7], (N_GROUPS, STATE), f32)
    A_im = math.pi * n[None, :] + 0.01 * jax.random.normal(ks[8], (N_GROUPS, STATE), f32)
    log_dt = jax.random.uniform(ks[9], (N_GROUPS,), f32, math.log(1e-3), math.log(1e-1))
    b_scale = (2.0 * GROUP) ** -0.5
    B_re = jax.random.normal(ks[10], (N_GROUPS, STATE, GROUP), f32) * b_scale
    B_im = jax.random.normal(ks[11], (N_GROUPS, STATE, GROUP), f32) * b_scale
    c_scale = (2.0 * STATE) ** -0.5
    C_re = jax.random.normal(ks[12], (N_GROUPS, GROUP, STATE), f32) * c_scale
    C_im = jax.random.normal(ks[13], (N_GROUPS, GROUP, STATE), f32) * c_scale
    D_skip = jax.random.normal(ks[14], (N_GROUPS, GROUP), f32)
    w_glu = jax.random.normal(ks[15], (SSM_W, 2 * SSM_W), f32) * SSM_W ** -0.5
    b_glu = 0.01 * jax.random.normal(ks[16], (2 * SSM_W,), f32)
    w_ssm_proj = jax.random.normal(ks[17], (SSM_W, D_MODEL), f32) * SSM_W ** -0.5
    w_out = jax.random.normal(ks[18], (D_MODEL, D_MODEL), f32) * D_MODEL ** -0.5
    return {"x": x, "norm_w": norm_w, "w_in": w_in, "q_norm_w": q_norm_w,
            "k_norm_w": k_norm_w, "sinks": sinks, "w_attn_proj": w_attn_proj,
            "A_re": A_re, "A_im": A_im, "log_dt": log_dt, "B_re": B_re, "B_im": B_im,
            "C_re": C_re, "C_im": C_im, "D_skip": D_skip, "w_glu": w_glu,
            "b_glu": b_glu, "w_ssm_proj": w_ssm_proj, "w_out": w_out}

def second_block(x, norm_w, w_in, q_norm_w, k_norm_w, sinks, w_attn_proj, A_re, A_im,
              log_dt, B_re, B_im, C_re, C_im, D_skip, w_glu, b_glu, w_ssm_proj, w_out):
    b, l, _ = x.shape
    split_pts = list(np.cumsum(IN_SIZES)[:-1])
    f32 = jnp.float32
    for _layer in range(DEPTH):
        h = rms_norm(x, norm_w)
        proj = h @ w_in
        q, k, v, a_gate, u, z, g_a, g_s = jnp.split(proj, split_pts, axis=-1)
        q = rms_norm(q.reshape(b, l, N_Q_HEADS, HEAD_DIM_2), q_norm_w)
        k = rms_norm(k.reshape(b, l, N_KV_HEADS, HEAD_DIM_2), k_norm_w)
        v = v.reshape(b, l, N_KV_HEADS, HEAD_DIM_2)
        attn = sliding_window_attention(q, k, v, sinks)
        y_a = (attn * jax.nn.silu(a_gate)) @ w_attn_proj
        u_g = u.reshape(b, l, N_GROUPS, GROUP).astype(f32)
        y_ssm = s5_ssm(u_g, A_re.astype(f32), A_im.astype(f32), log_dt.astype(f32),
                       B_re.astype(f32), B_im.astype(f32), C_re.astype(f32),
                       C_im.astype(f32), D_skip.astype(f32))
        y_ssm = jax.nn.gelu(y_ssm.reshape(b, l, SSM_W)).astype(x.dtype)
        glu_a, glu_b = jnp.split(y_ssm @ w_glu + b_glu, 2, axis=-1)
        y_s = (glu_a * jax.nn.sigmoid(glu_b) * jax.nn.silu(z)) @ w_ssm_proj
        merged = jax.nn.sigmoid(g_a) * y_a + jax.nn.sigmoid(g_s) * y_s
        x = x + merged @ w_out
    return x


def setup_inputs(seed=0):
    out = dict(first_inputs(seed))
    for name, value in second_inputs(seed + 1).items():
        if name != "x":
            out[name + "_2"] = value
    return out


def reference(
    x, c, ada_w, ada_b, norm1_g, w_in, cmp_pos_k, cmp_w1_k, cmp_w2_k, cmp_pos_v, cmp_w1_v,
    cmp_w2_v, lru_conv_w, lru_conv_b, lru_wa, lru_ba, lru_wi, lru_bi, lru_lambda, proj_a,
    proj_b, w_out, norm2_g, ffn_up, ffn_conv_w, ffn_conv_b, ffn_down, final_g, norm_w_2, w_in_2,
    q_norm_w_2, k_norm_w_2, sinks_2, w_attn_proj_2, A_re_2, A_im_2, log_dt_2, B_re_2, B_im_2,
    C_re_2, C_im_2, D_skip_2, w_glu_2, b_glu_2, w_ssm_proj_2, w_out_2,
):
    x = first_block(
        x, c, ada_w, ada_b, norm1_g, w_in, cmp_pos_k, cmp_w1_k, cmp_w2_k, cmp_pos_v, cmp_w1_v,
        cmp_w2_v, lru_conv_w, lru_conv_b, lru_wa, lru_ba, lru_wi, lru_bi, lru_lambda, proj_a,
        proj_b, w_out, norm2_g, ffn_up, ffn_conv_w, ffn_conv_b, ffn_down, final_g,
    )
    return second_block(
        x, norm_w_2, w_in_2, q_norm_w_2, k_norm_w_2, sinks_2, w_attn_proj_2, A_re_2, A_im_2,
        log_dt_2, B_re_2, B_im_2, C_re_2, C_im_2, D_skip_2, w_glu_2, b_glu_2, w_ssm_proj_2,
        w_out_2,
    )


_drawn_inputs = setup_inputs


def setup_inputs(seed=0):
    import zlib

    import numpy as np

    out = dict(_drawn_inputs(seed))
    spreads = {}
    factors = {'norm1_g': 8.0,
     'cmp_pos_k': 8.0,
     'cmp_w1_k': 4.682,
     'cmp_w2_k': 4.649,
     'cmp_pos_v': 8.0,
     'lru_conv_b': 8.0,
     'lru_wa': 2.946,
     'lru_ba': 8.0,
     'lru_bi': 8.0,
     'norm2_g': 8.0,
     'ffn_conv_b': 8.0,
     'final_g': 2.786,
     'norm_w_2': 8.0,
     'q_norm_w_2': 8.0,
     'k_norm_w_2': 8.0,
     'sinks_2': 29.683,
     'A_re_2': 64.0,
     'A_im_2': 64.0,
     'log_dt_2': 64.0,
     'B_re_2': 64.0,
     'B_im_2': 64.0,
     'C_re_2': 64.0,
     'C_im_2': 64.0,
     'b_glu_2': 54.356}
    for name, (base, spread) in spreads.items():
        noise = np.random.default_rng([zlib.crc32(name.encode()), seed]).standard_normal(out[name].shape)
        drawn = base * np.exp(spread * noise) if base else spread * noise
        out[name] = jnp.asarray(drawn.astype(out[name].dtype))
    for name, factor in factors.items():
        out[name] = (out[name] * factor).astype(out[name].dtype)
    return out
```

```python
from contextlib import ExitStack

import concourse.bass as bass
from concourse import mybir

F32 = mybir.dt.float32
F32R = mybir.dt.float32r
ACT = mybir.ActivationFunctionType
ALU = mybir.AluOpType
AX = mybir.AxisListType

P = 128
T = 256
D = 2048
DC = D // P
EPS = 1e-6
NEG = -1e30
N_CMP = 15
FF = 3 * D
FFC = FF // P
CB = 512
UK = 2
RAW = 4
RING = 4
LEAD = 3

VEC_SIZES = [("c", 16), ("ada_b", 96), ("norm1_g", 16), ("norm2_g", 16), ("final_g", 16), ("norm_w_2", 16),
             ("lru_conv_w", 64), ("lru_conv_b", 16), ("lru_ba", 16), ("lru_bi", 16), ("lru_lambda", 16),
             ("ffn_conv_w", 144), ("ffn_conv_b", 48), ("cmp_pos_k", 32), ("cmp_pos_v", 32), ("q_norm", 1),
             ("k_norm", 1), ("sinks", 16), ("A_re", 32), ("A_im", 32), ("log_dt", 32), ("D_skip", 8),
             ("b_glu", 16)]
VEC = {}
_at = 0
for _name, _n in VEC_SIZES:
    VEC[_name] = _at
    _at += _n
NVEC = _at


class Lin:

    def __init__(self, c, terms=()):
        self.c, self.terms = c, tuple(terms)

    def __add__(self, n):
        return Lin(self.c + n, self.terms)

    def over(self, reg, mult):
        return self if isinstance(reg, int) else Lin(self.c, self.terms + ((reg, mult),))

    def div(self, n):
        assert all(m % n == 0 for _, m in self.terms)
        return Lin(self.c // n, [(r, m // n) for r, m in self.terms])

    def value(self, mult=1, plus=0):
        v = self.c * mult + plus
        for r, m in self.terms:
            v = r * (m * mult) + v
        return v


class Group:

    def __init__(self, kind, w, col, slots, x, mode="T", width=CB):
        self.kind, self.w, self.col, self.slots, self.x, self.mode, self.width = kind, w, col, slots, x, mode, width


class Phase:
    def __init__(self, name, count, groups):
        self.name, self.count, self.groups = name, count, groups
        self.units = sum(2 * g.slots for g in groups)
        assert count == 1 or (self.units % 8 == 0 and len(groups) % 2 == 0)


def phases():
    G = Group
    ada = lambda first, step: G("ada", "ada_w", lambda i: (first + step * i) * CB if isinstance(i, int) else i * (step * CB) + first * CB, 4, "c", "ADA")
    lin = lambda kind, w, at, x, slots=4: G(kind, w, lambda i, at=at: i * CB + at, slots, x)
    out = [Phase("ada0", 1, [ada(0, 0), ada(1, 0)]),
           Phase("ada1", 3, [ada(2, 2), ada(3, 2)]),
           Phase("cmp", 1, [lin("kc", "w_in", 2048, "h"), lin("vc", "w_in", 2560, "h")]),
           Phase("kv", 2, [G("k", "w_in", lambda i: i * 1024 + 3072, 4, "h"),
                           G("v", "w_in", lambda i: i * 1024 + 3584, 4, "h", "N")]),
           Phase("gates", 1, [G("gates", "w_in", lambda i: 5120, 1, "h", "GATES", 48)]),
           Phase("nsa", 4, [lin("q", "w_in", 0, "h"), ada(8, 1)]),
           Phase("lru", 4, [lin("lx", "w_in", 5168, "h"), lin("ly", "w_in", 7216, "h"), ada(12, 1), ada(16, 1)]),
           Phase("merge", 4, [lin("ga", "w_in", 9264, "h"), lin("pa", "proj_a", 0, "oa"),
                              lin("gb", "w_in", 11312, "h"), lin("pb", "proj_b", 0, "ob")]),
           Phase("out", 4, [lin("wout", "w_out", 0, "h"), ada(20, 1)])]
    for half in range(2):
        out.append(Phase(f"up{half}", 6, [lin("gate", "ffn_up", half * FF // 2, "h"),
                                          lin("val", "ffn_up", FF + half * FF // 2, "h")]))
        down = lambda j, half=half: G("down", f"ffn_down{half}", lambda i: i * (2 * CB) + j * CB, 6, "hid")
        out.append(Phase(f"down{half}", 2, [down(0), down(1)]))
    at = dict(q=0, k=1024, v=1280, ag=1536, u=2560, z=3584, ga=4608, gs=6656)
    out += [Phase("uq", 2, [lin("u2", "w_in_2", at["u"], "h"), lin("q2", "w_in_2", at["q"], "h")]),
            Phase("kv2", 1, [G("k2", "w_in_2", lambda i: at["k"], 4, "h", "T", 256),
                             G("v2", "w_in_2", lambda i: at["v"], 4, "h", "N", 256)]),
            Phase("az", 2, [lin("ag2", "w_in_2", at["ag"], "h"), lin("z2", "w_in_2", at["z"], "h")]),
            Phase("glu", 2, [lin("gluA", "w_glu_2", 0, "ys", 2), lin("gluB", "w_glu_2", 1024, "ys", 2)]),
            Phase("merge2", 4, [lin("ga", "w_in_2", at["ga"], "h"), lin("pa", "w_attn_proj_2", 0, "at", 2),
                                lin("gb", "w_in_2", at["gs"], "h"), lin("pb", "w_ssm_proj_2", 0, "sg", 2)]),
            Phase("out2a", 1, [G("wout2", "w_out_2", lambda i: 0, 4, "h"), G("wout2", "w_out_2", lambda i: CB, 4, "h")]),
            Phase("out2b", 1, [G("wout2", "w_out_2", lambda i: 2 * CB, 4, "h"),
                               G("wout2", "w_out_2", lambda i: 3 * CB, 4, "h")])]
    return out


def build_program(nc, ctx, xT, vecs, W, small, outT):
    base = 16640
    spans = {}

    def put(name, at, shape, dt=F32):
        size = 4
        for n in shape[1:]:
            size *= n
        assert base + at + size <= nc.sbuf_usable_end, name
        spans[name] = (at, at + size)
        return nc.alloc_sbuf_tensor_at(name, list(shape), dt, offset=base + at)

    K = 1024
    rH, rA, rB, rM, rW = 0, 32 * K, 64 * K, 96 * K, 112 * K
    rWh, rWl, rEV, rT, rS = rW + 32 * K, rW + 48 * K, rW + 64 * K, rW + 72 * K, rW + 80 * K
    h = (put("h_hi", rH, [P, DC, T], F32R), put("h_lo", rH + 16 * K, [P, DC, T], F32R))
    oa = (put("oa_hi", rA, [P, DC, T], F32R), put("oa_lo", rA + 16 * K, [P, DC, T], F32R))
    ob = (put("ob_hi", rB, [P, DC, T], F32R), put("ob_lo", rB + 16 * K, [P, DC, T], F32R))
    res = put("res", rM, [P, DC, T])
    hid = (put("hid_hi", rA, [P, 24, T], F32R), put("hid_lo", rA + 24 * K, [P, 24, T], F32R))
    wraw = put("wraw", rW, [P, RAW, 2048])
    whi = put("whi", rWh, [P, RING, 1024], F32R)
    wlo = put("wlo", rWl, [P, RING, 1024], F32R)
    ev = put("ev", rEV, [P, 2, 4, T])
    t1 = put("t1", rT, [P, 4, T])
    t2 = put("t2", rT + 4 * K, [P, 4, T])
    k2 = put("k2", rB, [P, 2, 4, T])
    v2 = put("v2", rB + 8 * K, [P, 2, 2, 512])
    kc4 = put("kc4", rB + 16 * K, [P, 4, T])
    blocks = put("blocks", rB + 20 * K, [P, 32, 60])
    hidc = put("hidc", rB + 28 * K, [P, 2, 64])
    kcmp = put("kcmp", rB + 29 * K, [P, 64])
    vcmp = put("vcmp", rB + 30 * K, [P, 4, P])
    kg = put("kg", rM, [P, 2, T])
    vg = put("vg", rM + 2 * K, [P, 2, 2, P])
    kcg = put("kcg", rM + 4 * K, [P, 16])
    vcg = put("vcg", rM + 4 * K + 256, [P, P])
    pct = put("pct", rM + 5 * K, [16, 4, T])
    sm = put("sm", rM + 9 * K, [P, 2, T])
    pt = put("pt", rM + 11 * K, [P, 2, 384])
    pc = put("pc", rM + 14 * K, [P, 4, 16])
    st = put("st", rM + 14 * K + 512, [P, 64])
    wcmp = put("wcmp", rA, [P, 32, P])
    q4 = t1
    lr = put("lr", rM, [P, 4, T])
    li = put("li", rM + 4 * K, [P, 4, T])
    la = put("la", rM + 8 * K, [P, 4, T])
    lt = put("lt", rM + 12 * K, [P, 4, T])
    u_2 = put("u_2", rA, [P, 8, T])
    q_2 = put("q_2", rA + 8 * K, [P, 8, T])
    ag_2 = put("ag_2", rA + 16 * K, [P, 8, T])
    k_2 = put("k_2", rA + 24 * K, [P, 2, T])
    v_2 = put("v_2", rA + 28 * K, [P, 2, T])
    z_2 = put("z_2", rB, [P, 8, T])
    at_ = (put("at_hi", rB + 8 * K, [P, 8, T], F32R), put("at_lo", rB + 16 * K, [P, 8, T], F32R))
    ys = (put("ys_hi", rA + 8 * K, [P, 8, T], F32R), put("ys_lo", rA + 16 * K, [P, 8, T], F32R))
    sg = (put("sg_hi", rA, [P, 8, T], F32R), put("sg_lo", rA + 24 * K, [P, 8, T], F32R))
    mg2 = put("mg2", rA + 8 * K, [P, DC, T])
    kg2 = put("kg2", rB + 24 * K, [P, T])
    vg2 = put("vg2", rB + 25 * K, [P, 2, 64])
    qg2 = put("qg2", rB + 26 * K, [P, 2, T])
    sm2 = put("sm2", rB + 28 * K, [P, T])
    pt2 = put("pt2", rB + 29 * K, [P, 384])
    ph = put("ph", rB + 24 * K, [P, 4, 32, 16])
    ssb = [put(f"ssb{n}", rA + 24 * K + 2 * K * n, [P, 2, T]) for n in range(4)] + \
          [put(f"sst{n}", rT + 2 * K * n, [P, 2, T]) for n in range(4)]
    vec = put("vec", rS, [P, NVEC])
    off = rS + (NVEC * 4 + 63) // 64 * 64
    mod = put("mod", off, [P, 96]); off += 384
    adat = put("adat", off, [P, 4]); off += 64
    gates = put("gates", off, [P, 2, 48]); off += 384
    ones = put("ones", off, [P, P]); off += 512
    halves = put("halves", off, [P, P]); off += 512
    ident = put("ident", off, [P, P]); off += 512
    causal = put("causal", off, [P, 2, T]); off += 2048
    band = put("band", off, [P, T]); off += 1024
    cmask = put("cmask", off, [P, 2, 16]); off += 128
    cadd = put("cadd", off, [P, 2, 16]); off += 128
    rstd = put("rstd", off, [P, T]); off += 1024
    cc = put("cc", off, [P, DC, 2], F32R); off += 128
    cs = put("cs", off, [P, 2, DC]); off += 128
    scA = put("scA", off, [P, DC]); off += 64
    l8 = put("l8", off, [P, DC]); off += 64
    ltmp = put("ltmp", off, [P, 4, DC]); off += 256
    w2 = put("w2", rM, [P, 2, P])
    ssp = put("ssp", off, [P, 5, 32]); off += 640
    wgate = put("wgate", off, [P, 2, 4, P])
    bz = put("bz", off, [P, 2, P])
    cz = put("cz", off + 1024, [P, 2, 4, 32])
    cz2 = put("cz2", off + 2048, [P, 2, 4, 32])
    uc = put("uc", off + 3072, [P, T])

    def V(name, n=0, w=1):
        return vec[:, VEC[name] + n:VEC[name] + n + w]

    def Vd(name, at, w=1):
        return vec[:, bass.ds(at + VEC[name], w)]

    pairs = [ctx.enter_context(nc.psum_tensor(f"pair{n}", [P, 4, T], F32)) for n in range(2)]
    bank = [ctx.enter_context(nc.psum_tensor(f"bank{n}", [P, 2, T], F32)) for n in range(4)]

    def sem(name):
        return ctx.enter_context(nc.semaphore(name))

    w_loaded = [sem(f"w_loaded{n}") for n in range(RAW)]
    hi_ready, lo_ready, pe_units = sem("hi_ready"), sem("lo_ready"), sem("pe_units")
    evacuated, ev_used = sem("evacuated"), sem("ev_used")
    consts_in, consts_made, x_in = sem("consts_in"), sem("consts_made"), sem("x_in")
    x_back = sem("x_back")
    residual_done = sem("residual_done")
    to_act, to_pe, to_pool = sem("dve_to_act"), sem("dve_to_pe"), sem("dve_to_pool")
    act_to_dve, act_to_pe = sem("act_to_dve"), sem("act_to_pe")
    pe_to_dve, pe_to_act = sem("pe_to_dve"), sem("pe_to_act")
    pool_to_pe = sem("pool_to_pe")
    pool_dma = sem("pool_dma")
    stored = sem("stored")
    S = dict(to_act=to_act, to_pe=to_pe, to_pool=to_pool, act_to_dve=act_to_dve, act_to_pe=act_to_pe,
             pe_to_dve=pe_to_dve, pe_to_act=pe_to_act, pool_to_pe=pool_to_pe, pool_dma=pool_dma)

    X = {"h": h, "oa": oa, "ob": ob, "hid": hid, "ys": ys, "at": at_, "sg": sg}
    PH = phases()
    N_UNITS = sum(ph.units * ph.count for ph in PH)
    block = ctx.enter_context(nc.Block())

    class Tally:

        def __init__(self):
            self.n = {k: Lin({"to_pe": 1, "act_to_dve": 2, "to_pool": 1}.get(k, 0)) for k in S}

        def step(self, key, k=1):
            self.n[key] = self.n[key] + k
            return self.n[key].value()

    def grown(run):
        j, fresh = Job(None, None, Tally()), Tally()
        run(j)
        return {k: j.t.n[k].c - fresh.n[k].c for k in S}

    def repeat(j, count, run, body):
        start, grow = dict(j.t.n), grown(lambda d: run(d, 0))

        def once(i):
            for k in S:
                j.t.n[k] = start[k].over(i, grow[k])
            body(i)

        if count == 1:
            once(0)
        elif j.me in ("pool",) and not any(grow[k] for k in ("pool_dma", "pool_to_pe")):
            pass
        else:
            with j.eng.Fori(0, count) as i:
                once(i)
        for k in S:
            j.t.n[k] = Lin(start[k].c + grow[k] * count)

    def walk(me, eng, unit, group_end):
        j = Job(me, eng, Tally())
        u, g = Lin(0), Lin(0)
        for ph in PH:
            before(ph, j)

            def body(i, ph=ph, u=u, g=g):
                uu, gg = u.over(i, ph.units), g.over(i, len(ph.groups))
                for gr in ph.groups:
                    for n in range(2 * gr.slots):
                        unit(ph, gr, uu, gg, n, i)
                        uu = uu + 1
                    group_end(ph, gr, uu, gg, i)
                    side(ph, gr, i, j)
                    gg = gg + 1

            repeat(j, ph.count, lambda d, i, ph=ph: [side(ph, gr, i, d) for gr in ph.groups], body)
            u, g = u + ph.units * ph.count, g + len(ph.groups) * ph.count

    def nothing(*a):
        pass


    class Job:
        def __init__(self, me, eng, tally):
            self.me, self.eng, self.t = me, eng, tally

        def sync(self, key, frm, to, ins=None, k=1):
            v = self.t.step(key, k)
            if self.me == frm:
                ins.then_inc(S[key], k)
            if self.me == to:
                self.eng.wait_ge(S[key], v)

    ve, sc, te, po = nc.vector, nc.scalar, nc.tensor, nc.gpsimd

    def split(dst, at, n, src, eng=None):
        hi, lo = dst
        ve.tensor_copy(hi[:, bass.ds(at, n), :], src)
        ve.drain()
        return ve.tensor_tensor(lo[:, bass.ds(at, n), :], src, hi[:, bass.ds(at, n), :].bitcast(F32), ALU.subtract)

    def norm(j, gain_scale, gain_shift, in_place):
        me = j.me
        for c in range(0, DC, 4):
            tt = (t1, t2)[c // 4 % 2]
            ins = None
            if me == "dve":
                if c >= 8:
                    j.eng.wait_ge(pe_to_dve, sq_read[c // 4 - 2])
                ins = ve.tensor_tensor(tt[:, :, :], res[:, c:c + 4, :], res[:, c:c + 4, :], ALU.mult)
            j.sync("to_pe", "dve", "pe", ins)
            if me == "pe":
                for n in range(4):
                    ins = te.matmul(bank[0][:, 0, :], ones[:, :], tt[:, n, :], start=(c + n == 0),
                                    stop=(c + n == DC - 1))
                ins.then_inc(pe_to_dve, 1)
            v = j.t.step("pe_to_dve")
            if c == 0:
                sq_read = []
            sq_read.append(v)
        ins = None
        if me == "dve":
            j.eng.wait_ge(pe_to_dve, sq_read[-1])
            ins = ve.tensor_scalar(rstd[:, :], bank[0][:, 0, :], 1.0 / D, EPS, ALU.mult, ALU.add)
        j.sync("to_act", "dve", "act", ins)
        if me == "act":
            ins = sc.activation(rstd[:, :], rstd[:, :], ACT.Sqrt)
        j.sync("act_to_dve", "act", "dve", ins)
        if me == "dve":
            ve.reciprocal(rstd[:, :], rstd[:, :])
            if gain_shift is not None:
                ve.scalar_tensor_tensor(out=scA[:, :], in0=mod[:, gain_scale[1]:gain_scale[1] + DC], scalar=1.0,
                                        in1=V(gain_scale[0], 0, DC), op0=ALU.add, op1=ALU.mult)
            else:
                ve.tensor_copy(scA[:, :], V(gain_scale[0], 0, DC))
            ve.drain()
            for c in range(0, DC, 4):
                tt = (t1, t2)[c // 4 % 2] if not in_place else res[:, c:c + 4, :]
                rs = rstd[:, :].unsqueeze(1).broadcast_to([P, 4, T])
                ve.tensor_tensor(tt[:, :, :], res[:, c:c + 4, :], rs, ALU.mult)
                ve.drain()
                for n in range(4):
                    if gain_shift is not None:
                        ve.tensor_scalar(tt[:, n, :], tt[:, n, :], scA[:, c + n:c + n + 1],
                                         mod[:, gain_shift + c + n:gain_shift + c + n + 1], ALU.mult, ALU.add)
                    else:
                        ve.tensor_scalar(tt[:, n, :], tt[:, n, :], scA[:, c + n:c + n + 1], None, ALU.mult)
                ve.drain()
                if not in_place:
                    split(h, c, 4, tt[:, :, :])
                    ve.drain()

    def ready(j):
        ins = ve.drain() if j.me == "dve" else None
        j.sync("to_pe", "dve", "pe", ins)

    def compress(j, which):
        me = j.me
        pos = "cmp_pos_k" if which == 0 else "cmp_pos_v"
        ins = None
        if me == "dve":
            view = kc4[:, :, :]
            for l in range(32):
                ve.tensor_scalar(blocks[:, l, :].rearrange("p (g n) -> p g n", g=4),
                                 kc4[:, :, l:l + 225:16], V(pos, l), None, ALU.add)
            ins = ve.drain()
        j.sync("to_pe", "dve", "pe", ins)
        if me == "pool":
            j.eng.wait_ge(to_pe, j.t.n["to_pe"].value(1, -1 if which == 0 else 0))
            if which == 1:
                j.eng.wait_ge(pe_to_dve, COMP_PE[0])
            po.dma_start(wcmp[:, :, :], small["cmp_w1"][which].rearrange("l d e -> d l e")).then_inc(pool_dma, 16)
            po.dma_start(w2[:, which, :], small["cmp_w2"][which]).then_inc(pool_dma, 16)
        v = j.t.step("pool_dma", 32)
        if me == "pe":
            j.eng.wait_ge(pool_dma, v)
            for l in range(32):
                ins = te.matmul(bank[1][:, 0, 0:60], wcmp[:, l, :], blocks[:, l, :], start=(l == 0), stop=(l == 31))
            ins.then_inc(pe_to_act, 1)
        v = j.t.step("pe_to_act")
        if me == "act":
            j.eng.wait_ge(pe_to_act, v)
            ins = sc.activation(hidc[:, which, 0:60], bank[1][:, 0, 0:60], ACT.Gelu_apprx_tanh)
        j.sync("act_to_pe", "act", "pe", ins)
        if me == "pe":
            if which == 0:
                ins = te.matmul(bank[2][:, 0, 0:60], w2[:, 0, :], hidc[:, 0, 0:60], start=True, stop=True)
            else:
                for g in range(4):
                    ins = te.matmul(bank[2][0:N_CMP, :, :].rearrange("p a b -> p (a b)")[:, g * P:(g + 1) * P],
                                    hidc[:, 1, g * N_CMP:(g + 1) * N_CMP], w2[:, 1, :], start=True, stop=True)
            ins.then_inc(pe_to_dve, 1)
        v = j.t.step("pe_to_dve")
        COMP_PE[which] = v
        if me == "dve":
            j.eng.wait_ge(pe_to_dve, v)
            if which == 0:
                ve.tensor_copy(kcmp[:, 0:60], bank[2][:, 0, 0:60])
            else:
                ve.tensor_copy(vcmp[0:N_CMP, :, :].rearrange("p a b -> p (a b)"),
                               bank[2][0:N_CMP, :, :].rearrange("p a b -> p (a b)"))
            ve.drain()

    COMP_PE = {}

    def nsa(j, i):
        me = j.me
        SCALE = float(P) ** -0.5
        ins = None
        if me == "dve":
            ins = ve.drain()
        j.sync("to_pool", "dve", "pool", ins)
        if me == "pool":
            po.tensor_copy(kg[:, :, :], k2[:, :, bass.ds(i, 1), :].rearrange("p a o t -> p a (o t)"))
            for br in range(2):
                po.tensor_copy(vg[:, br, :, :], v2[:, br, :, bass.ts(i, P)])
            po.tensor_copy(kcg[:, 0:N_CMP], kcmp[:, bass.ts(i, N_CMP)])
            po.tensor_copy(vcg[0:N_CMP, :], vcmp[0:N_CMP, bass.ds(i, 1), :].rearrange("p o d -> p (o d)"))
            ins = po.drain()
        j.sync("pool_to_pe", "pool", "pe", ins)
        for b in range(2):
            if me == "pe":
                for hd in range(4):
                    ins = te.matmul(bank[3][:, b, 16 * hd:16 * hd + N_CMP], q4[:, hd, b * P:(b + 1) * P],
                                    kcg[:, 0:N_CMP], start=True, stop=True)
            j.sync("pe_to_dve", "pe", "dve", ins)
            sv = pc[:, :, 0:N_CMP]
            if me == "dve":
                src = bank[3][:, b, 0:64].rearrange("p (h n) -> p h n", h=4)[:, :, 0:N_CMP]
                add = cadd[:, b, 0:N_CMP].unsqueeze(1).broadcast_to([P, 4, N_CMP])
                mul = cmask[:, b, 0:N_CMP].unsqueeze(1).broadcast_to([P, 4, N_CMP])
                ve.scalar_tensor_tensor(out=sv, in0=src, scalar=SCALE, in1=add, op0=ALU.mult, op1=ALU.add)
                ve.drain()
                ve.tensor_reduce(st[:, 0:4], sv, AX.X, ALU.max)
                ve.drain()
                ve.tensor_tensor(sv, sv, st[:, 0:4].unsqueeze(2).broadcast_to([P, 4, N_CMP]), ALU.subtract)
                ins = ve.drain()
            j.sync("to_act", "dve", "act", ins)
            if me == "act":
                ins = sc.activation(sv, sv, ACT.Exp)
            j.sync("act_to_dve", "act", "dve", ins)
            if me == "dve":
                ve.tensor_tensor(sv, sv, mul, ALU.mult)
                ve.drain()
                ve.tensor_reduce(st[:, 4:8], sv, AX.X, ALU.add)
                ve.drain()
                ve.tensor_scalar(st[:, 8:12], st[:, 4:8], 1e-30, None, ALU.max)
                ve.drain()
                ve.reciprocal(st[:, 12:16], st[:, 8:12])
                ve.drain()
                for hd in range(4):
                    ve.tensor_tensor(st[:, 16 + hd:17 + hd], st[:, 12 + hd:13 + hd], gates[:, b, bass.ds(i * 12 + 3 * hd, 1)], ALU.mult)
                ve.drain()
                ins = ve.tensor_tensor(sv, sv, st[:, 16:20].unsqueeze(2).broadcast_to([P, 4, N_CMP]), ALU.mult)
            j.sync("to_pe", "dve", "pe", ins)
            if me == "pe":
                for hd in range(4):
                    ins = te.transpose(bank[1 + hd // 2][0:N_CMP, hd % 2, b * P:(b + 1) * P], pc[:, hd, 0:N_CMP],
                                       ident[:, :])
            j.sync("pe_to_act", "pe", "act", ins)
            if me == "act":
                for hd2 in range(2):
                    ins = sc.activation(pct[0:N_CMP, 2 * hd2:2 * hd2 + 2, b * P:(b + 1) * P],
                                        bank[1 + hd2][0:N_CMP, :, b * P:(b + 1) * P], ACT.Copy)
            j.sync("act_to_pe", "act", "pe", ins)
        for hd in range(4):
            for b in range(2):
                w = P * (b + 1)
                if me == "pe":
                    for br in range(2):
                        ins = te.matmul(bank[0][:, br, 0:w], q4[:, hd, b * P:(b + 1) * P], kg[:, br, 0:w],
                                        start=True, stop=True)
                j.sync("pe_to_dve", "pe", "dve", ins)
                if me == "dve":
                    mask = causal[:, b, 0:w].unsqueeze(1).broadcast_to([P, 2, w])
                    ve.scalar_tensor_tensor(out=sm[:, :, 0:w], in0=bank[0][:, :, 0:w], scalar=SCALE, in1=mask,
                                            op0=ALU.mult, op1=ALU.add)
                    ve.drain()
                    ve.tensor_reduce(st[:, 20:22], sm[:, :, 0:w], AX.X, ALU.max)
                    ve.drain()
                    ins = ve.tensor_scalar(st[:, 22:24], st[:, 20:22], -1.0, None, ALU.mult)
                j.sync("to_act", "dve", "act", ins)
                if me == "act":
                    for br in range(2):
                        ins = sc.activation(sm[:, br, 0:w], sm[:, br, 0:w], ACT.Exp, bias=st[:, 22 + br:23 + br],
                                            accum_out=st[:, 24 + br:25 + br])
                j.sync("act_to_dve", "act", "dve", ins)
                if me == "dve":
                    ve.reciprocal(st[:, 26:28], st[:, 24:26])
                    ve.drain()
                    ve.tensor_tensor(st[:, 28:30], st[:, 26:28], gates[:, b, bass.ds(i * 12 + 3 * hd + 1, 2)],
                                     ALU.mult)
                    ve.drain()
                    for br in range(2):
                        ins = ve.tensor_scalar(sm[:, br, 0:w], sm[:, br, 0:w], st[:, 28 + br:29 + br], None, ALU.mult)
                j.sync("to_pe", "dve", "pe", ins)
                if me == "pe":
                    for br in range(2):
                        for m in range(b + 1):
                            ins = te.transpose(
                                bank[1 + br][:, :, :].rearrange("p a b -> p (a b)")[:, (m + b) * P:(m + b + 1) * P],
                                sm[:, br, m * P:(m + 1) * P], ident[:, :])
            j.sync("pe_to_act", "pe", "act", ins)
            if me == "act":
                for br in range(2):
                    ins = sc.activation(pt[:, br, :], bank[1 + br][:, :, :].rearrange("p a b -> p (a b)")[:, 0:384],
                                        ACT.Copy)
            j.sync("act_to_pe", "act", "pe", ins)
            if me == "pe":
                te.matmul(bank[3][:, 0, :], vcg[0:N_CMP, :], pct[0:N_CMP, hd, :], start=True, stop=False,
                          skip_group_check=True)
                for br in range(2):
                    te.matmul(bank[3][:, 0, :], vg[:, br, 0, :], pt[:, br, 0:T], start=False, stop=False,
                              skip_group_check=True)
                    ins = te.matmul(bank[3][:, 0, P:T], vg[:, br, 1, :], pt[:, br, T:384], start=False,
                                    stop=(br == 1), skip_group_check=True)
            j.sync("pe_to_dve", "pe", "dve", ins)
            if me == "dve":
                split(oa, i * 4 + hd, 1, bank[3][:, 0:1, :])
                ve.drain()

    def conv(dst, src, taps, wname, bname, ci, stride):
        for n in range(4):
            ve.tensor_scalar(dst[:, n, :], src[:, n, :], Vd(wname, ci + ((taps - 1) * stride + n)),
                             Vd(bname, ci + n), ALU.mult, ALU.add)
        for s in range(1, taps):
            ve.drain()
            for n in range(4):
                last = ve.scalar_tensor_tensor(out=dst[:, n, s:T], in0=src[:, n, 0:T - s],
                                               scalar=Vd(wname, ci + ((taps - 1 - s) * stride + n)),
                                               in1=dst[:, n, s:T], op0=ALU.mult, op1=ALU.add)
        return last

    def lru(j, i):
        me = j.me
        ins = None
        if me == "dve":
            ins = ve.drain()
        j.sync("to_pe", "dve", "pe", ins)
        if me == "pool":
            j.eng.wait_ge(to_pe, j.t.n["to_pe"].value())
            po.dma_start(wgate[:, 0, :, :], small["lru_wa"][bass.ts(i, 4)].rearrange("c d e -> d c e")).then_inc(pool_dma, 16)
            po.dma_start(wgate[:, 1, :, :], small["lru_wi"][bass.ts(i, 4)].rearrange("c d e -> d c e")).then_inc(pool_dma, 16)
        v = j.t.step("pool_dma", 32)
        if me == "pe":
            j.eng.wait_ge(pool_dma, v)
            for a in range(2):
                for n in range(4):
                    ins = te.matmul(bank[2 * a + n // 2][:, n % 2, :], wgate[:, a, n, :], t1[:, n, :],
                                    start=True, stop=True)
        j.sync("pe_to_act", "pe", "act", ins)
        if me == "act":
            for a, dst, bname in ((0, lr, "lru_ba"), (1, li, "lru_bi")):
                for n in range(4):
                    ins = sc.activation(dst[:, n, :], bank[2 * a + n // 2][:, n % 2, :], ACT.Sigmoid,
                                        bias=Vd(bname, i * 4 + n))
            sc.drain()
            for n in range(4):
                sc.activation(lt[:, n, :], lr[:, n, :], ACT.Tanh, scale=l8[:, bass.ds(i * 4 + n, 1)])
            for n in range(4):
                ins = sc.activation(la[:, n, :], lr[:, n, :], ACT.Exp, scale=l8[:, bass.ds(i * 4 + n, 1)])
        j.sync("act_to_dve", "act", "dve", ins)
        if me == "dve":
            ve.tensor_tensor(li[:, :, :], li[:, :, :], t1[:, :, :], ALU.mult)
            ve.tensor_tensor(lr[:, :, :], la[:, :, :], la[:, :, :], ALU.mult)
            ve.drain()
            ins = ve.scalar_tensor_tensor(out=lt[:, :, :].rearrange("p a b -> p (a b)"),
                                          in0=lr[:, :, :].rearrange("p a b -> p (a b)"), scalar=1.0,
                                          in1=lt[:, :, :].rearrange("p a b -> p (a b)"), op0=ALU.add, op1=ALU.mult)
        j.sync("to_act", "dve", "act", ins)
        if me == "act":
            ins = sc.activation(lt[:, :, :], lt[:, :, :], ACT.Sqrt, scale=-1.0)
        j.sync("act_to_dve", "act", "dve", ins)
        if me == "dve":
            ve.tensor_tensor(li[:, :, :], li[:, :, :], lt[:, :, :], ALU.mult)
            ve.drain()
            for n in range(4):
                ve.tensor_tensor_scan(out=lr[:, n, :], data0=la[:, n, :], data1=li[:, n, :], initial=0.0,
                                      op0=ALU.mult, op1=ALU.add)
            ve.drain()
            ve.tensor_tensor(lr[:, :, :], lr[:, :, :], t2[:, :, :], ALU.mult)
            ve.drain()
            split(ob, i * 4, 4, lr[:, :, :])
            ve.drain()

    def head_norm(j, src, n):
        me = j.me
        ins = ve.tensor_tensor(t1[:, 0:n, :], src, src, ALU.mult) if me == "dve" else None
        j.sync("to_pe", "dve", "pe", ins)
        if me == "pe":
            for c in range(n):
                ins = te.matmul(bank[c // 2][:, c % 2, :], halves[:, :], t1[:, c, :], start=True, stop=True)
        j.sync("pe_to_dve", "pe", "dve", ins)
        if me == "dve":
            for c in range(0, n, 2):
                ve.tensor_scalar(t2[:, c:c + 2, :], bank[c // 2][:, :, :], 1.0 / 64, EPS, ALU.mult, ALU.add)
            ins = ve.drain()
        j.sync("to_act", "dve", "act", ins)
        if me == "act":
            ins = sc.activation(t2[:, 0:n, :], t2[:, 0:n, :], ACT.Sqrt)
        j.sync("act_to_dve", "act", "dve", ins)
        if me == "dve":
            ve.reciprocal(t2[:, 0:n, :], t2[:, 0:n, :])
            ve.drain()
            ve.tensor_tensor(t2[:, 0:n, :], src, t2[:, 0:n, :], ALU.mult)
            ve.drain()

    def attention2_pair(j, pair):
        for e in range(2):
            attention2(j, pair, e)

    def attention2(j, pair, e):
        me = j.me
        ins, g = None, pair * 2 + e
        if me == "dve":
            for half in range(2):
                ve.tensor_copy(kg2[64 * half:64 * half + 64, :].unsqueeze(1),
                               k_2[64 * e:64 * e + 64, bass.ds(pair, 1), :])
            ins = ve.drain()
        j.sync("to_pool", "dve", "pool", ins)
        if me == "pool":
            po.tensor_copy(vg2[:, :, :], v_2[:, :, bass.ts(g, 64)])
            po.tensor_copy(qg2[:, :, :], q_2[:, bass.ts(g, 2), :])
            ins = po.drain()
        j.sync("pool_to_pe", "pool", "pe", ins)
        for hd in range(4):
            r = slice(64 * (hd % 2), 64 * (hd % 2) + 64)
            for b in range(2):
                w = P * (b + 1)
                if me == "pe":
                    ins = te.matmul(bank[0][:, 0, 0:w], qg2[r, hd // 2, b * P:(b + 1) * P], kg2[r, 0:w],
                                    start=True, stop=True)
                j.sync("pe_to_dve", "pe", "dve", ins)
                if me == "dve":
                    mask = causal[:, 0, 0:w] if b == 0 else band[:, :]
                    sink = Vd("sinks", g * 4 + hd)
                    ve.scalar_tensor_tensor(out=sm2[:, 0:w], in0=bank[0][:, 0, 0:w], scalar=0.125, in1=mask,
                                            op0=ALU.mult, op1=ALU.add)
                    ve.drain()
                    ve.tensor_reduce(st2[:, 0:1], sm2[:, 0:w], AX.X, ALU.max)
                    ve.drain()
                    ve.tensor_tensor(st2[:, 1:2], st2[:, 0:1], sink, ALU.max)
                    ve.drain()
                    ve.tensor_scalar(st2[:, 2:3], st2[:, 1:2], -1.0, None, ALU.mult)
                    ve.tensor_tensor(st2[:, 3:4], sink, st2[:, 1:2], ALU.subtract)
                    ins = ve.drain()
                j.sync("to_act", "dve", "act", ins)
                if me == "act":
                    sc.activation(st2[:, 4:5], st2[:, 3:4], ACT.Exp)
                    ins = sc.activation(sm2[:, 0:w], sm2[:, 0:w], ACT.Exp, bias=st2[:, 2:3], accum_out=st2[:, 5:6])
                j.sync("act_to_dve", "act", "dve", ins)
                if me == "dve":
                    ve.tensor_tensor(st2[:, 6:7], st2[:, 4:5], st2[:, 5:6], ALU.add)
                    ve.drain()
                    ve.reciprocal(st2[:, 7:8], st2[:, 6:7])
                    ve.drain()
                    ins = ve.tensor_scalar(sm2[:, 0:w], sm2[:, 0:w], st2[:, 7:8], None, ALU.mult)
                j.sync("to_pe", "dve", "pe", ins)
                if me == "pe":
                    for m in range(b + 1):
                        ins = te.transpose(bank[1][:, :, :].rearrange("p a b -> p (a b)")[:, (m + b) * P:(m + b + 1) * P],
                                           sm2[:, m * P:(m + 1) * P], ident[:, :])
            j.sync("pe_to_act", "pe", "act", ins)
            if me == "act":
                ins = sc.activation(pt2[:, :], bank[1][:, :, :].rearrange("p a b -> p (a b)")[:, 0:384], ACT.Copy)
            j.sync("act_to_pe", "act", "pe", ins)
            if me == "pe":
                te.matmul(bank[3][r, 0, :], vg2[:, 0, :], pt2[:, 0:T], start=True, stop=False, skip_group_check=True)
                ins = te.matmul(bank[3][r, 0, P:T], vg2[:, 1, :], pt2[:, T:384], start=False, stop=True,
                                skip_group_check=True)
            if hd % 2:
                j.sync("pe_to_dve", "pe", "dve", ins)
                if me == "dve":
                    ve.tensor_tensor(t1[:, 0:1, :], bank[3][:, 0:1, :], ag_2[:, bass.ds(g * 2 + hd // 2, 1), :], ALU.mult)
                    ve.drain()
                    split(at_, g * 2 + hd // 2, 1, t1[:, 0:1, :])
                    ve.drain()

    st2 = ltmp[:, 0, :]
    MAG, CFR, CFI, W1, W2 = (ssp[:, n, :] for n in range(5))

    def cmul(o_re, o_im, a_re, a_im, b_re, b_im, x, y, conj=False):
        ve.tensor_tensor(x, a_re, b_re, ALU.mult)
        ve.tensor_tensor(y, a_im, b_im, ALU.mult)
        ve.drain()
        ve.tensor_tensor(o_re, x, y, ALU.add if conj else ALU.subtract)
        ve.drain()
        ve.tensor_tensor(x, a_re, b_im, ALU.mult)
        ve.tensor_tensor(y, a_im, b_re, ALU.mult)
        ve.drain()
        last = ve.tensor_tensor(o_im, x, y, ALU.subtract if conj else ALU.add)
        ve.drain()
        return last

    def ssm_tables(j):
        me = j.me
        dt_, th, rr, s1, c1, x, y = (ssb[n][:, a, 0:32] for n, a in ((0, 0), (0, 1), (1, 0), (1, 1), (2, 0), (2, 1), (3, 0)))
        ins = None
        if me == "dve":
            ins = ve.drain()
        j.sync("to_act", "dve", "act", ins)
        if me == "act":
            ins = sc.activation(dt_, V("log_dt", 0, 32), ACT.Exp)
        j.sync("act_to_dve", "act", "dve", ins)
        if me == "dve":
            ve.tensor_tensor(th, dt_, V("A_im", 0, 32), ALU.mult)
            ve.tensor_tensor(x, dt_, V("A_re", 0, 32), ALU.mult)
            ve.drain()
            magic = 12582912.0
            two_pi = 6.283185307179586
            p1 = 6.28125
            p2 = 0.0019350051879882812
            p3 = two_pi - p1 - p2
            ve.tensor_scalar(y, th, 1.0 / two_pi, None, ALU.mult)
            ve.drain()
            ve.tensor_scalar(y, y, magic, None, ALU.add)
            ve.drain()
            ve.tensor_scalar(y, y, -magic, None, ALU.add)
            ve.drain()
            ve.tensor_copy(rr, th)
            ve.drain()
            for part in (p1, p2, p3):
                ve.scalar_tensor_tensor(out=rr, in0=y, scalar=-part, in1=rr, op0=ALU.mult, op1=ALU.add)
                ve.drain()
            ve.tensor_scalar(rr, rr, 0.5, None, ALU.mult)
            ve.drain()
            ins = ve.tensor_scalar(c1, rr, -1.0, two_pi / 4, ALU.mult, ALU.add)
            ve.drain()
            ve.tensor_scalar(rr, rr, -3.1415925, 3.1415925, ALU.max, ALU.min)
            ins = ve.tensor_scalar(c1, c1, -3.1415925, 3.1415925, ALU.max, ALU.min)
            ins = ve.drain()
        j.sync("to_act", "dve", "act", ins)
        if me == "act":
            sc.activation(MAG, x, ACT.Exp)
            sc.activation(s1, rr, ACT.Sin)
            ins = sc.activation(W2, c1, ACT.Sin)
        j.sync("act_to_dve", "act", "dve", ins)
        if me == "dve":
            ve.tensor_tensor(x, s1, W2, ALU.mult)
            ve.tensor_tensor(y, s1, s1, ALU.mult)
            ve.drain()
            ve.tensor_scalar(s1, x, 2.0, None, ALU.mult)
            ve.tensor_scalar(c1, y, -2.0, 1.0, ALU.mult, ALU.add)
            ve.drain()
            ve.tensor_tensor(x, MAG, c1, ALU.mult)
            ve.tensor_tensor(dt_, MAG, s1, ALU.mult)
            ve.tensor_tensor(th, V("A_re", 0, 32), V("A_re", 0, 32), ALU.mult)
            ve.tensor_tensor(rr, V("A_im", 0, 32), V("A_im", 0, 32), ALU.mult)
            ve.drain()
            ve.tensor_scalar(x, x, -1.0, None, ALU.add)
            ve.tensor_tensor(th, th, rr, ALU.add)
            ve.drain()
            ve.reciprocal(th, th)
            ve.drain()
            cmul(CFR, CFI, V("A_re", 0, 32), V("A_im", 0, 32), x, dt_, W1, W2, conj=True)
            ve.tensor_tensor(CFR, CFR, th, ALU.mult)
            ve.tensor_tensor(CFI, CFI, th, ALU.mult)
            ve.drain()
            er, ei, e2r, e2i = c1, s1, dt_, th
            wx = ssb[4 + 0][:, :, :].rearrange("p a b -> p (a b)")
            wy = ssb[4 + 1][:, :, :].rearrange("p a b -> p (a b)")
            for half in range(2):
                re, im = ph[:, 2 * half, :, :], ph[:, 2 * half + 1, :, :]
                ve.memset(re[:, :, 0:1], 1.0)
                ve.memset(im[:, :, 0:1], 0.0)
                ve.drain()
                L = 1
                while L < 16:
                    br = er.unsqueeze(2).broadcast_to([P, 32, L])
                    bi = ei.unsqueeze(2).broadcast_to([P, 32, L])
                    wxl = wx[:, 0:32 * L].rearrange("p (a b) -> p a b", b=L)
                    wyl = wy[:, 0:32 * L].rearrange("p (a b) -> p a b", b=L)
                    cmul(re[:, :, L:2 * L], im[:, :, L:2 * L], re[:, :, 0:L], im[:, :, 0:L], br, bi, wxl, wyl)
                    cmul(e2r, e2i, er, ei, er, ei, wx[:, 0:32], wy[:, 0:32])
                    er, ei, e2r, e2i = e2r, e2i, er, ei
                    L *= 2

    def ssm(j, m):
        me = j.me
        ins = None
        if me == "dve":
            ins = ve.drain()
        j.sync("to_pool", "dve", "pool", ins)
        if me == "pool":
            po.dma_start(bz[:, :, :], small["B"][bass.ds(m, 1)].rearrange("o p c s -> p (o c) s")).then_inc(pool_dma, 16)
            po.dma_start(cz[:, :, :, :], small["C"][bass.ds(m, 1)].rearrange("o p c q k -> p (o c) q k")).then_inc(pool_dma, 16)
            po.tensor_copy(uc[:, :].unsqueeze(1), u_2[:, bass.ds(m, 1), :])
            ins = po.drain()
        j.sync("pool_to_pe", "pool", "pe", ins)
        v = j.t.step("pool_dma", 32)
        if me == "pe":
            j.eng.wait_ge(pool_dma, v)
            for q in range(4):
                for c in range(2):
                    ins = te.matmul(bank[q][:, c, :], bz[32 * q:32 * q + 32, c, :], uc[32 * q:32 * q + 32, :],
                                    start=True, stop=True)
        j.sync("pe_to_act", "pe", "act", ins)
        if me == "dve":
            j.eng.wait_ge(pool_dma, v)
            cr = CFR[:, bass.ts(m, 4)].unsqueeze(2).broadcast_to([P, 4, 32])
            ci = CFI[:, bass.ts(m, 4)].unsqueeze(2).broadcast_to([P, 4, 32])
            x = ssb[6][:, 0, 0:128].rearrange("p (a b) -> p a b", b=32)
            y = ssb[6][:, 1, 0:128].rearrange("p (a b) -> p a b", b=32)
            cmul(cz2[:, 0, :, :], cz2[:, 1, :, :], cz[:, 0, :, :], cz[:, 1, :, :], cr, ci, x, y)
            ve.tensor_scalar(cz2[:, 1, :, :], cz2[:, 1, :, :], -1.0, None, ALU.mult)
            ve.drain()
        for q2 in range(2):
            er, ei = ssb[0], ssb[1]
            br_, bi_ = ssb[2], ssb[3]
            x, y = ssb[6], ssb[7]
            wr, wi = ssb[4], ssb[5]
            if me == "act":
                for n in range(2):
                    sc.activation(br_[:, n, :], bank[2 * q2 + n][:, 0, :], ACT.Copy)
                    ins = sc.activation(bi_[:, n, :], bank[2 * q2 + n][:, 1, :], ACT.Copy)
            j.sync("act_to_dve", "act", "dve", ins)
            if me == "dve":
                f4 = lambda t: t[:, :, :].rearrange("p q (a b) -> p q a b", b=16)
                hi_ = lambda k: ph[:, 2 + k, bass.ds(m * 4 + 2 * q2, 2), :].unsqueeze(3).broadcast_to([P, 2, 16, 16])
                lo_ = lambda k: ph[:, k, bass.ds(m * 4 + 2 * q2, 2), :].unsqueeze(2).broadcast_to([P, 2, 16, 16])
                cmul(f4(er), f4(ei), hi_(0), hi_(1), lo_(0), lo_(1), f4(x), f4(y))
                a3 = lambda t: t[:, :, :]
                cmul(a3(wr), a3(wi), a3(er), a3(ei), a3(br_), a3(bi_), a3(x), a3(y), conj=True)
                for n in range(2):
                    mg = MAG[:, bass.ds(m * 4 + 2 * q2 + n, 1)].broadcast_to([P, T])
                    ve.tensor_tensor_scan(out=br_[:, n, :], data0=mg, data1=wr[:, n, :], initial=0.0,
                                          op0=ALU.mult, op1=ALU.add)
                    ve.tensor_tensor_scan(out=bi_[:, n, :], data0=mg, data1=wi[:, n, :], initial=0.0,
                                          op0=ALU.mult, op1=ALU.add)
                ve.drain()
                cmul(a3(wr), a3(wi), a3(er), a3(ei), a3(br_), a3(bi_), a3(x), a3(y))
                ins = ve.drain()
            j.sync("to_pe", "dve", "pe", ins)
            ins = ve.drain() if me == "dve" else None
            j.sync("to_act", "dve", "act", ins)
            if me == "pe":
                for n in range(2):
                    q = 2 * q2 + n
                    te.matmul(pairs[0][32 * q:32 * q + 32, 0, :], cz2[:, 0, q, :], wr[:, n, :], start=True,
                              stop=False, skip_group_check=True)
                    ins = te.matmul(pairs[0][32 * q:32 * q + 32, 0, :], cz2[:, 1, q, :], wi[:, n, :], start=False,
                                    stop=True, skip_group_check=True)
            j.sync("pe_to_dve", "pe", "dve", ins)
        if me == "dve":
            ins = ve.scalar_tensor_tensor(out=ssb[6][:, 0, :], in0=uc[:, :], scalar=Vd("D_skip", m),
                                          in1=pairs[0][:, 0, :], op0=ALU.mult, op1=ALU.add)
        j.sync("to_act", "dve", "act", ins)
        if me == "act":
            ins = sc.activation(ssb[6][:, 0, :], ssb[6][:, 0, :], ACT.Gelu_apprx_tanh)
        j.sync("act_to_dve", "act", "dve", ins)
        if me == "dve":
            split(ys, m, 1, ssb[6][:, 0:1, :])
            ve.drain()

    def before(ph, j):
        me, eng = j.me, j.eng
        if ph.name == "cmp":
            norm(j, ("norm1_g", 16), 0, False)
            if me == "dve":
                log_decay()
            ready(j)
        elif ph.name == "merge":
            ready(j)
        elif ph.name == "out":
            if me == "dve":
                for c in range(0, DC, 4):
                    split(h, c, 4, res[:, c:c + 4, :])
            ready(j)
            if me == "pool":
                eng.wait_ge(to_pe, j.t.n["to_pe"].value())
                po.dma_start(res[:, :, :], xT.rearrange("(c p) t -> p c t", p=P)).then_inc(x_back, 16)
            if me == "dve":
                eng.wait_ge(x_back, 16)
        elif ph.name == "up0":
            norm(j, ("norm2_g", 64), 48, False)
            ready(j)
        elif ph.name in ("down0", "down1", "merge2"):
            ready(j)
        elif ph.name == "uq":
            norm(j, ("final_g", 0), None, True)
            norm(j, ("norm_w_2", 0), None, False)
            ready(j)
        elif ph.name == "glu":
            repeat(j, 2, attention2_pair, lambda i: attention2_pair(j, i))
            ssm_tables(j)
            repeat(j, 8, ssm, lambda i: ssm(j, i))
            ready(j)
        elif ph.name == "out2a":
            if me == "dve":
                for c in range(0, DC, 4):
                    split(h, c, 4, mg2[:, c:c + 4, :])
            ready(j)

    def log_decay():
        z, s, s2, acc = ltmp[:, 3, :], ltmp[:, 0, :], ltmp[:, 1, :], ltmp[:, 2, :]
        ve.tensor_scalar(s2, z, 2.0, None, ALU.add)
        ve.drain()
        ve.reciprocal(s2, s2)
        ve.drain()
        ve.tensor_tensor(s, z, s2, ALU.mult)
        ve.drain()
        ve.tensor_tensor(s2, s, s, ALU.mult)
        ve.memset(acc, 1.0 / 19)
        ve.drain()
        for n in range(17, 0, -2):
            ve.tensor_tensor(acc, acc, s2, ALU.mult)
            ve.drain()
            ve.tensor_scalar(acc, acc, 1.0 / n, None, ALU.add)
            ve.drain()
        ve.tensor_tensor(acc, acc, s, ALU.mult)
        ve.tensor_scalar(z, V("lru_lambda", 0, DC), 0.0, 8.0, ALU.min, ALU.mult)
        ve.drain()
        ve.scalar_tensor_tensor(out=l8[:, :], in0=acc, scalar=-16.0, in1=z, op0=ALU.mult, op1=ALU.add)
        ve.drain()

    def side(ph, gr, i, j):
        me = j.me
        if gr.kind == "kc":
            compress(j, 0)
        elif gr.kind == "vc":
            compress(j, 1)
        elif ph.name == "nsa" and gr.kind == "ada":
            nsa(j, i)
        elif ph.name == "lru" and gr is ph.groups[3]:
            lru(j, i)
        elif gr.kind == "gate":
            ins = ve.drain() if me == "dve" else None
            j.sync("to_act", "dve", "act", ins)
            if me == "act":
                ins = sc.activation(t1[:, :, :], t1[:, :, :], ACT.Gelu_apprx_tanh)
            j.sync("act_to_dve", "act", "dve", ins)
        elif gr.kind in ("q2", "k2"):
            dst, name = (q_2[:, bass.ts(i, 4), :], "q_norm") if gr.kind == "q2" else (k_2[:, :, :], "k_norm")
            n = 4 if gr.kind == "q2" else 2
            head_norm(j, dst, n)
            if me == "dve":
                ve.tensor_scalar(dst, t2[:, 0:n, :], V(name), None, ALU.mult)
                ve.drain()

    @block.sync
    def _(sp):
        sp.dma_start(vec[:, :], vecs).then_inc(consts_in, 16)
        sp.dma_start(res[:, :, :], xT.rearrange("(c p) t -> p c t", p=P)).then_inc(x_in, 16)

        def unit(ph, gr, u, g, n, i):
            if n % 2:
                return
            slot = (u.c // 2) % RAW
            col = gr.col(i)
            if not isinstance(col, int) and n == 0:
                sp.lower_val(col * 4)
            if u.c >= 2 * RAW:
                sp.wait_ge(lo_ready, u.value(1, 2 - 2 * RAW))
            if gr.mode == "GATES":
                src = W[gr.w][:, gr.col(i):gr.col(i) + 48].rearrange("(k p) n -> p k n", p=P)
                dst = wraw[:, slot, 0:DC * 48].rearrange("p (k n) -> p k n", n=48)
                sp.dma_start(dst, src).then_inc(w_loaded[slot], 16)
                return
            k0 = n * UK * P
            rows = W[gr.w][k0:k0 + 4 * P, :].rearrange("(k p) n -> p k n", p=P)
            dst = wraw[:, slot, :].rearrange("p (k n) -> p k n", k=4)
            sp.dma_start(dst[:, :, 0:gr.width], rows[:, :, bass.ds(col, gr.width)]).then_inc(w_loaded[slot], 16)

        walk("sp", sp, unit, nothing)
        sp.wait_ge(residual_done, 1)
        sp.dma_start(outT.rearrange("(c p) t -> p c t", p=P), res[:, :, :]).then_inc(stored, 16)
        sp.wait_ge(stored, 16)

    def split_act(u, act):
        slot, half, r = (u.c // 2) % RAW, u.c % 2, u.c % RING
        act.wait_ge(w_loaded[slot], u.div(2 * RAW).value(16, 16))
        if u.c >= RING:
            act.wait_ge(pe_units, u.value(1, 1 - RING))
        sc.activation(whi[:, r, :], wraw[:, slot, 1024 * half:1024 * half + 1024], ACT.Copy).then_inc(hi_ready, 1)

    EVAC = {"ga": ACT.Sigmoid, "gb": ACT.Sigmoid, "ly": ACT.Gelu_apprx_tanh, "gates": ACT.Sigmoid,
            "ag2": ACT.Silu, "z2": ACT.Silu}

    @block.scalar
    def _(act):
        act.wait_ge(consts_in, 16)
        sc.activation(cs[:, 0, :], V("c", 0, DC), ACT.Silu).then_inc(act_to_dve, 1)
        sc.activation(ltmp[:, 3, :], V("lru_lambda", 0, DC), ACT.Abs)
        sc.drain()
        sc.activation(ltmp[:, 3, :], ltmp[:, 3, :], ACT.Exp, scale=-1.0).then_inc(act_to_dve, 1)
        for n in range(LEAD):
            split_act(Lin(n), act)

        def unit(ph, gr, u, g, n, i):
            if u.terms or u.c + LEAD < N_UNITS:
                split_act(u + LEAD, act)

        def group_end(ph, gr, u, g, i):
            p = g.c % 2
            act.wait_ge(pe_units, u.value())
            if g.c >= 2:
                act.wait_ge(ev_used, g.value(1, -1))
            if gr.mode == "ADA":
                ins = sc.activation(ev[:, p, 0:2, :], pairs[p][:, 0:2, :], ACT.Copy)
            elif gr.mode == "GATES":
                ins = sc.activation(gates[:, :, :], pairs[p][:, 0:4:2, 0:48], ACT.Sigmoid)
            elif gr.kind == "k2":
                ins = sc.activation(ev[:, p, 0:2, :], pairs[p][:, 0:2, :], ACT.Copy)
            elif gr.kind == "v2":
                ins = sc.activation(ev[:, p, 0:4:2, :], pairs[p][:, 0:4:2, :], ACT.Copy)
            elif gr.kind in EVAC:
                ins = sc.activation(ev[:, p, :, :], pairs[p][:, :, :], EVAC[gr.kind])
            elif gr.kind == "gluB":
                for n in range(4):
                    ins = sc.activation(ev[:, p, n, :], pairs[p][:, n, :], ACT.Sigmoid, bias=Vd("b_glu", i * 4 + (8 + n)))
            else:
                ins = sc.activation(ev[:, p, :, :], pairs[p][:, :, :], ACT.Copy)
            ins.then_inc(evacuated, 1)

        walk("act", act, unit, group_end)

    def ada_at(ph, gr, i):
        n = ph.groups.index(gr)
        first, step = {"ada0": (4 * n, 0), "ada1": (8 + 4 * n, 8), "nsa": (32, 4), "lru": (48 + 16 * (n - 2), 4),
                       "out": (80, 4)}[ph.name]
        return i * step + first

    def split_dve(u, dve):
        slot, half, r = (u.c // 2) % RAW, u.c % 2, u.c % RING
        dve.wait_ge(hi_ready, u.value(1, 1))
        ve.tensor_tensor(wlo[:, r, :], wraw[:, slot, 1024 * half:1024 * half + 1024], whi[:, r, :].bitcast(F32),
                         ALU.subtract).then_inc(lo_ready, 1)

    @block.vector
    def _(dve):
        ve.memset(ones[:, :], 1.0).then_inc(to_pool, 1)
        ve.memset(halves[:, :], 0.0)
        ve.drain()
        ve.memset(halves[0:64, 0:64], 1.0)
        ve.memset(halves[64:128, 64:128], 1.0)
        ve.drain()
        dve.wait_ge(act_to_dve, 2)
        ve.tensor_copy(cc[:, :, 0:1].rearrange("p a b -> p (a b)"), cs[:, 0, :])
        ve.drain()
        ve.tensor_tensor(cc[:, :, 1:2].rearrange("p a b -> p (a b)"), cs[:, 0, :],
                         cc[:, :, 0:1].rearrange("p a b -> p (a b)").bitcast(F32), ALU.subtract).then_inc(to_pe, 1)
        dve.wait_ge(x_in, 16)
        dve.wait_ge(consts_in, 16)
        dve.wait_ge(consts_made, 1)
        for n in range(LEAD):
            split_dve(Lin(n), dve)

        def unit(ph, gr, u, g, n, i):
            if u.terms or u.c + LEAD < N_UNITS:
                split_dve(u + LEAD, dve)

        def group_end(ph, gr, u, g, i):
            p = g.c % 2
            e = ev[:, p, :, :]
            dve.wait_ge(evacuated, g.value(1, 1))
            k = gr.kind
            fl = lambda t: t.rearrange("p a b -> p (a b)")
            done = None
            if k == "ada":
                cols = ada_at(ph, gr, i)
                row = ev[:, p, 0:2, :].rearrange("p a (c n) -> p (a c) n", n=P)
                ve.tensor_tensor(row, row, ident[:, :].unsqueeze(1).broadcast_to([P, 4, P]), ALU.mult)
                ve.drain()
                done = ve.tensor_reduce(adat[:, :], row, AX.X, ALU.add)
                ve.drain()
                ve.tensor_tensor(mod[:, bass.ds(cols, 4)], adat[:, :], Vd("ada_b", cols, 4), ALU.add)
            elif k in ("kc", "vc"):
                done = ve.tensor_copy(kc4[:, :, :], e)
            elif k == "k":
                done = ve.tensor_copy(k2[:, bass.ds(i, 1), :, :].rearrange("p o g t -> p (o g) t"), e)
            elif k == "v":
                done = ve.tensor_copy(v2[:, bass.ds(i, 1), :, :].rearrange("p o a b -> p (o a b)"), fl(e))
            elif k == "gates":
                done = ve.drain()
            elif k == "q":
                done = ve.tensor_copy(q4[:, :, :], e)
            elif k == "lx":
                done = conv(t1, e, 4, "lru_conv_w", "lru_conv_b", i * 4, DC)
            elif k == "ly":
                done = ve.tensor_copy(t2[:, :, :], e)
            elif k in ("ga", "gb"):
                done = ve.tensor_copy(t1[:, :, :], e)
            elif k == "pa":
                m = res if ph.name == "merge" else mg2
                done = ve.tensor_tensor(m[:, bass.ts(i, 4), :], t1[:, :, :], e, ALU.mult)
            elif k == "pb":
                m = res if ph.name == "merge" else mg2
                done = ve.tensor_tensor(t2[:, :, :], t1[:, :, :], e, ALU.mult)
                ve.drain()
                ve.tensor_tensor(m[:, bass.ts(i, 4), :], m[:, bass.ts(i, 4), :], t2[:, :, :], ALU.add)
            elif k in ("wout", "down"):
                g0 = 32 if k == "wout" else 80
                for n in range(4):
                    c = i * 4 + n if k == "wout" else i * 8 + (4 * ph.groups.index(gr) + n)
                    done = ve.scalar_tensor_tensor(out=res[:, bass.ds(c, 1), :].rearrange("p o t -> p (o t)"),
                                                   in0=e[:, n, :], scalar=mod[:, bass.ds(c + g0, 1)],
                                                   in1=res[:, bass.ds(c, 1), :].rearrange("p o t -> p (o t)"),
                                                   op0=ALU.mult, op1=ALU.add)
            elif k == "wout2":
                c = gr.col(0) // P
                done = ve.tensor_tensor(res[:, c:c + 4, :], res[:, c:c + 4, :], e, ALU.add)
            elif k == "gate":
                first = 24 if ph.name == "up1" else 0
                done = conv(t1, e, 3, "ffn_conv_w", "ffn_conv_b", i * 4 + first, FFC)
            elif k == "val":
                done = ve.tensor_tensor(t2[:, :, :], t1[:, :, :], e, ALU.mult)
                ve.drain()
                split(hid, i * 4, 4, t2[:, :, :])
            elif k == "u2":
                done = ve.tensor_copy(u_2[:, bass.ts(i, 4), :], e)
            elif k == "q2":
                done = ve.tensor_copy(q_2[:, bass.ts(i, 4), :], e)
            elif k == "k2":
                done = ve.tensor_copy(k_2[:, :, :], ev[:, p, 0:2, :])
            elif k == "v2":
                done = ve.tensor_copy(v_2[:, :, :], ev[:, p, 0:4:2, :])
            elif k == "ag2":
                done = ve.tensor_copy(ag_2[:, bass.ts(i, 4), :], e)
            elif k == "z2":
                done = ve.tensor_copy(z_2[:, bass.ts(i, 4), :], e)
            elif k == "gluA":
                for n in range(4):
                    done = ve.scalar_tensor_tensor(out=t1[:, n, :], in0=e[:, n, :], scalar=Vd("b_glu", i * 4 + n),
                                                   in1=z_2[:, bass.ds(i * 4 + n, 1), :].rearrange("p o t -> p (o t)"),
                                                   op0=ALU.add, op1=ALU.mult)
            elif k == "gluB":
                done = ve.tensor_tensor(t2[:, :, :], t1[:, :, :], e, ALU.mult)
                ve.drain()
                split(sg, i * 4, 4, t2[:, :, :])
            done.then_inc(ev_used, 1)
            ve.drain()

        walk("dve", dve, unit, group_end)
        ve.drain().then_inc(residual_done, 1)

    @block.tensor
    def _(pe):
        pe.wait_ge(to_pe, 1)
        pe.wait_ge(consts_made, 1)

        def unit(ph, gr, u, g, n, i):
            r = u.c % RING
            pair = pairs[g.c % 2]
            if n == 0 and g.c >= 2:
                pe.wait_ge(evacuated, g.value(1, -1))
            pe.wait_ge(lo_ready, u.value(1, 1))
            K = 2 * UK * gr.slots
            if gr.mode == "ADA":
                for kk in range(UK):
                    k = n * UK + kk
                    for t, (w, part) in enumerate(((whi, 0), (whi, 1), (wlo, 0))):
                        ins = te.matmul(pair[:, 0:2, :].rearrange("p a b -> p (a b)"),
                                        cc[:, k, part:part + 1].broadcast_to([P, P]), w[:, r, kk * CB:(kk + 1) * CB],
                                        start=(k == 0 and t == 0), stop=(k == K - 1 and t == 2))
            elif gr.mode == "T":
                whv = whi[:, r, :].rearrange("p (k n) -> p k n", k=UK)
                wlv = wlo[:, r, :].rearrange("p (k n) -> p k n", k=UK)
                hi, lo = X[gr.x]
                for kk in range(UK):
                    k = n * UK + kk
                    for o in range(gr.width // P):
                        for t, (w, x) in enumerate(((whv, hi), (whv, lo), (wlv, hi))):
                            ins = te.matmul(pair[:, o, :], w[:, kk, o * P:(o + 1) * P], x[:, k, :],
                                            start=(k == 0 and o % 2 == 0 and t == 0),
                                            stop=(k == K - 1 and t == 2), skip_group_check=True)
            else:
                hi, lo = X[gr.x]
                if gr.mode == "GATES":
                    ks, wd = DC * (n == 0), 48
                    ins = pe.drain() if n else None
                else:
                    ks, wd = UK, gr.width
                for kk in range(ks):
                    k = n * ks + kk
                    if gr.mode == "GATES":
                        view = lambda w: w[:, r, kk * 48:(kk + 1) * 48]
                    else:
                        view = lambda w: w[:, r, kk * 512:kk * 512 + wd]
                    for b in range(2):
                        for t, (w, x) in enumerate(((whi, hi), (whi, lo), (wlo, hi))):
                            dst = pair[:, 2 * b:2 * b + 2, :].rearrange("p a b -> p (a b)")[:, 0:wd]
                            ins = te.matmul(dst, x[:, k, b * P:(b + 1) * P], view(w), start=(k == 0 and t == 0),
                                            stop=(k == 15 and t == 2))
            ins.then_inc(pe_units, 1)

        walk("pe", pe, unit, nothing)

    @block.gpsimd
    def _(pool):
        pool.wait_ge(to_pool, 1)
        po.memset(causal[:, :, :], 0.0)
        po.memset(band[:, :], 0.0)
        po.memset(cmask[:, :, :], 1.0)
        po.memset(cadd[:, :, :], 0.0)
        po.drain()
        po.affine_select(out=causal[:, :, :], in_=causal[:, :, :], compare_op=ALU.is_ge, fill=NEG, base=0,
                         pattern=[[P, 2], [-1, T]], channel_multiplier=1)
        po.affine_select(out=band[:, :], in_=band[:, :], compare_op=ALU.is_ge, fill=NEG, base=-1,
                         pattern=[[1, T]], channel_multiplier=-1)
        po.affine_select(out=cmask[:, :, :], in_=cmask[:, :, :], compare_op=ALU.is_ge, fill=0.0, base=-31,
                         pattern=[[P, 2], [-16, 16]], channel_multiplier=1)
        po.affine_select(out=cadd[:, :, :], in_=cadd[:, :, :], compare_op=ALU.is_ge, fill=NEG, base=-31,
                         pattern=[[P, 2], [-16, 16]], channel_multiplier=1)
        po.affine_select(out=ident[:, :], in_=ones[:, :], compare_op=ALU.is_equal, fill=0.0, base=0,
                         pattern=[[-1, P]], channel_multiplier=1)
        po.drain()
        po.affine_select(out=band[:, :], in_=band[:, :], compare_op=ALU.is_ge, fill=NEG, base=P,
                         pattern=[[-1, T]], channel_multiplier=1)
        po.drain()
        po.drain().then_inc(consts_made, 1)
        walk("pool", pool, nothing, nothing)



def kernel(**inputs):
    import numpy as np
    import concourse.bacc as bacc
    from concourse.bass_utils import run_bass_kernel_spmd as run

    nc = bacc.Bacc("TRN2", target_bir_lowering=False, num_devices=1)
    arrays = {}

    def dram(name, a):
        a = np.ascontiguousarray(a)
        arrays[name + "_dram"] = a
        return nc.dram_tensor(name + "_dram", a.shape, F32, kind="ExternalInput").ap()

    v = {k: np.asarray(a) for k, a in inputs.items()}
    cols = lambda a: a.reshape(-1, P).T
    packed = {
        "c": cols(v["c"]), "ada_b": cols(v["ada_b"]), "norm1_g": cols(v["norm1_g"]), "norm2_g": cols(v["norm2_g"]),
        "final_g": cols(v["final_g"]), "norm_w_2": cols(v["norm_w_2"]), "lru_conv_w": cols(v["lru_conv_w"]),
        "lru_conv_b": cols(v["lru_conv_b"]), "lru_ba": cols(v["lru_ba"]), "lru_bi": cols(v["lru_bi"]),
        "lru_lambda": cols(v["lru_lambda"]), "ffn_conv_w": cols(v["ffn_conv_w"]), "ffn_conv_b": cols(v["ffn_conv_b"]),
        "cmp_pos_k": v["cmp_pos_k"][0].T, "cmp_pos_v": v["cmp_pos_v"][0].T,
        "q_norm": np.concatenate([v["q_norm_w_2"]] * 2)[:, None], "k_norm": np.concatenate([v["k_norm_w_2"]] * 2)[:, None],
        "sinks": np.broadcast_to(v["sinks_2"], (P, 16)), "A_re": cols(v["A_re_2"]), "A_im": cols(v["A_im_2"]),
        "log_dt": cols(np.repeat(v["log_dt_2"], 64)), "D_skip": cols(v["D_skip_2"]), "b_glu": cols(v["b_glu_2"]),
    }
    vecs = dram("vecs", np.concatenate([packed[name] for name, _ in VEC_SIZES], axis=1))
    xT = dram("xT", v["x"][0].T)
    W = {name: dram(name, v[name][0]) for name in ("ada_w", "w_in", "proj_a", "proj_b", "w_out", "ffn_up", "ffn_down")}
    W.update({name: dram(name, v[name]) for name in ("w_in_2", "w_attn_proj_2", "w_glu_2", "w_ssm_proj_2", "w_out_2")})
    W["ffn_down0"], W["ffn_down1"] = W["ffn_down"][0:FF // 2, :], W["ffn_down"][FF // 2:FF, :]
    B = np.zeros((8, 4, 2, 16, 2, 2, 64), np.float32)
    C = np.zeros((8, 2, 64, 2, 4, 2, 16), np.float32)
    for part, (b, c) in enumerate((("B_re_2", "C_re_2"), ("B_im_2", "C_im_2"))):
        b = v[b].reshape(8, 4, 2, 64, 16)
        c = v[c].reshape(8, 4, 2, 16, 64)
        for e in range(2):
            B[:, :, e, :, part, e, :] = b[:, :, e].transpose(0, 1, 3, 2)
            C[:, e, :, part, :, e, :] = c[:, :, e].transpose(0, 3, 1, 2)
    small = {
        "cmp_w1": [dram("cmp_w1_k", v["cmp_w1_k"][0]), dram("cmp_w1_v", v["cmp_w1_v"][0])],
        "cmp_w2": [dram("cmp_w2_k", v["cmp_w2_k"][0]), dram("cmp_w2_v", v["cmp_w2_v"][0])],
        "lru_wa": dram("lru_wa", v["lru_wa"][0]), "lru_wi": dram("lru_wi", v["lru_wi"][0]),
        "B": dram("B", B.reshape(8, P, 2, P)), "C": dram("C", C.reshape(8, P, 2, 4, 32)),
    }
    outT = nc.dram_tensor("outT_dram", (D, T), F32, kind="ExternalOutput").ap()
    with ExitStack() as ctx:
        build_program(nc, ctx, xT, vecs, W, small, outT)
    r = run(nc, [arrays], core_ids=[0])
    return np.ascontiguousarray(r.results[0]["outT_dram"].T)[None]
```

```python
from contextlib import ExitStack
from itertools import chain

import concourse.bass as bass
from concourse import mybir

F32 = mybir.dt.float32
F32R = mybir.dt.float32r
ACT = mybir.ActivationFunctionType
ALU = mybir.AluOpType
AX = mybir.AxisListType

P = 128
T = 256
D = 2048
DC = D // P
EPS = 1e-6
NEG = -1e30
N_CMP = 15
FF = 3 * D
FFC = FF // P
CB = 512
UK = 2
RAW = 4
RING = 4
LEAD = 3

VEC_SIZES = [("c", 16), ("ada_b", 96), ("norm1_g", 16), ("norm2_g", 16), ("final_g", 16), ("norm_w_2", 16),
             ("lru_conv_w", 64), ("lru_conv_b", 16), ("lru_ba", 16), ("lru_bi", 16), ("lru_lambda", 16),
             ("ffn_conv_w", 144), ("ffn_conv_b", 48), ("cmp_pos_k", 32), ("cmp_pos_v", 32), ("q_norm", 1),
             ("k_norm", 1), ("sinks", 16), ("A_re", 32), ("A_im", 32), ("log_dt", 32), ("D_skip", 8),
             ("b_glu", 16)]
VEC = {}
_at = 0
for _name, _n in VEC_SIZES:
    VEC[_name] = _at
    _at += _n
NVEC = _at


class Lin:

    def __init__(self, c, terms=()):
        self.c, self.terms = c, tuple(terms)

    def __add__(self, n):
        return Lin(self.c + n, self.terms)

    def over(self, reg, mult):
        return self if isinstance(reg, int) else Lin(self.c, self.terms + ((reg, mult),))

    def div(self, n):
        assert all(m % n == 0 for _, m in self.terms)
        return Lin(self.c // n, [(r, m // n) for r, m in self.terms])

    def value(self, mult=1, plus=0):
        v = self.c * mult + plus
        for r, m in self.terms:
            v = r * (m * mult) + v
        return v


class Group:

    def __init__(self, kind, w, col, slots, x, mode="T", width=CB):
        self.kind, self.w, self.col, self.slots, self.x, self.mode, self.width = kind, w, col, slots, x, mode, width


class Phase:
    def __init__(self, name, count, groups):
        self.name, self.count, self.groups = name, count, groups
        self.units = sum(2 * g.slots for g in groups)
        assert count == 1 or (self.units % 8 == 0 and len(groups) % 2 == 0)


def phases():
    G = Group
    ada = lambda first, step: G("ada", "ada_w", lambda i: (first + step * i) * CB if isinstance(i, int) else i * (step * CB) + first * CB, 4, "c", "ADA")
    lin = lambda kind, w, at, x, slots=4: G(kind, w, lambda i, at=at: i * CB + at, slots, x)
    out = [Phase("ada0", 1, [ada(0, 0), ada(1, 0)]),
           Phase("ada1", 3, [ada(2, 2), ada(3, 2)]),
           Phase("cmp", 1, [lin("kc", "w_in", 2048, "h"), lin("vc", "w_in", 2560, "h")]),
           Phase("kv", 2, [G("k", "w_in", lambda i: i * 1024 + 3072, 4, "h"),
                           G("v", "w_in", lambda i: i * 1024 + 3584, 4, "h", "N")]),
           Phase("gates", 1, [G("gates", "w_in", lambda i: 5120, 1, "h", "GATES", 48)]),
           Phase("q0", 1, [lin("q", "w_in", 0, "h")]),
           Phase("nsa", 3, [ada(8, 1), lin("q", "w_in", CB, "h")]),
           Phase("nsa3", 1, [ada(11, 0)]),
           Phase("lru", 4, [lin("lx", "w_in", 5168, "h"), lin("ly", "w_in", 7216, "h"), ada(12, 1), ada(16, 1)]),
           Phase("merge", 4, [lin("ga", "w_in", 9264, "h"), lin("pa", "proj_a", 0, "oa"),
                              lin("gb", "w_in", 11312, "h"), lin("pb", "proj_b", 0, "ob")]),
           Phase("out", 4, [lin("wout", "w_out", 0, "h"), ada(20, 1)])]
    for half in range(2):
        out.append(Phase(f"up{half}", 6, [lin("gate", "ffn_up", half * FF // 2, "h"),
                                          lin("val", "ffn_up", FF + half * FF // 2, "h")]))
        down = lambda j, half=half: G("down", f"ffn_down{half}", lambda i: i * (2 * CB) + j * CB, 6, "hid")
        out.append(Phase(f"down{half}", 2, [down(0), down(1)]))
    at = dict(q=0, k=1024, v=1280, ag=1536, u=2560, z=3584, ga=4608, gs=6656)
    out += [Phase("kv2", 1, [G("k2", "w_in_2", lambda i: at["k"], 4, "h", "T", 256),
                             G("v2", "w_in_2", lambda i: at["v"], 4, "h", "N", 256)]),
            Phase("qag", 2, [lin("q2", "w_in_2", at["q"], "h"), lin("ag2", "w_in_2", at["ag"], "h")]),
            Phase("uz", 2, [lin("u2", "w_in_2", at["u"], "h"), lin("z2", "w_in_2", at["z"], "h")]),
            Phase("attn_out", 2, [G(kind, w, lambda i, a=a, n=n: i * (2 * CB) + (a + n * CB), slots, x) for n in range(2)
                                  for kind, w, a, slots, x in (("ga", "w_in_2", at["ga"], 4, "h"),
                                                               ("pa", "w_attn_proj_2", 0, 2, "at"))]),
            Phase("gs", 2, [G("gs", "w_in_2", lambda i, n=n: i * (2 * CB) + (at["gs"] + n * CB), 4, "h") for n in range(2)]),
            Phase("glu", 2, [lin("gluA", "w_glu_2", 0, "ys", 2), lin("gluB", "w_glu_2", 1024, "ys", 2)]),
            Phase("ssm_out", 2, [G("ps", "w_ssm_proj_2", lambda i, n=n: i * (2 * CB) + n * CB, 2, "sg") for n in range(2)]),
            Phase("out2a", 1, [G("wout2", "w_out_2", lambda i: 0, 4, "h"), G("wout2", "w_out_2", lambda i: CB, 4, "h")]),
            Phase("out2b", 1, [G("wout2", "w_out_2", lambda i: 2 * CB, 4, "h"),
                               G("wout2", "w_out_2", lambda i: 3 * CB, 4, "h")])]
    return out


def build_program(nc, ctx, xT, vecs, W, small, outT):
    base = 16640
    spans = {}

    def put(name, at, shape, dt=F32):
        size = 4
        for n in shape[1:]:
            size *= n
        assert base + at + size <= nc.sbuf_usable_end, name
        spans[name] = (at, at + size)
        return nc.alloc_sbuf_tensor_at(name, list(shape), dt, offset=base + at)

    K = 1024
    rH, rA, rB, rM, rW = 0, 32 * K, 64 * K, 96 * K, 112 * K
    rWh, rWl, rEV, rT, rS = rW + 32 * K, rW + 48 * K, rW + 64 * K, rW + 72 * K, rW + 80 * K
    h = (put("h_hi", rH, [P, DC, T], F32R), put("h_lo", rH + 16 * K, [P, DC, T], F32R))
    oa = (put("oa_hi", rA, [P, DC, T], F32R), put("oa_lo", rA + 16 * K, [P, DC, T], F32R))
    ob = (put("ob_hi", rB, [P, DC, T], F32R), put("ob_lo", rB + 16 * K, [P, DC, T], F32R))
    res = put("res", rM, [P, DC, T])
    hid = (put("hid_hi", rA, [P, 24, T], F32R), put("hid_lo", rA + 24 * K, [P, 24, T], F32R))
    wraw = put("wraw", rW, [P, RAW, 2048])
    whi = put("whi", rWh, [P, RING, 1024], F32R)
    wlo = put("wlo", rWl, [P, RING, 1024], F32R)
    ev = put("ev", rEV, [P, 2, 4, T])
    t1 = put("t1", rT, [P, 4, T])
    t2 = put("t2", rT + 4 * K, [P, 4, T])
    k2 = put("k2", rB, [P, 2, 4, T])
    v2 = put("v2", rB + 8 * K, [P, 2, 2, 512])
    kc4 = put("kc4", rB + 16 * K, [P, 4, T])
    blocks = put("blocks", rB + 20 * K, [P, 32, 60])
    hidc = put("hidc", rB + 28 * K, [P, 2, 64])
    kcmp = put("kcmp", rB + 29 * K, [P, 64])
    vcmp = put("vcmp", rB + 30 * K, [P, 4, P])
    kg = put("kg", rM, [P, 2, T])
    vg = put("vg", rM + 2 * K, [P, 2, 2, P])
    kcg = put("kcg", rM + 4 * K, [P, 16])
    vcg = put("vcg", rM + 4 * K + 256, [P, P])
    pct = put("pct", rM + 5 * K, [16, 4, T])
    sm = put("sm", rM + 9 * K, [P, 2, T])
    pt = put("pt", rM + 11 * K, [P, 2, 384])
    pc = put("pc", rM + 14 * K, [P, 8, 16])
    st = put("st", rM + 14 * K + 512, [P, 64])
    sm0 = put("sm0", rM + 14 * K + 768, [P, 2, P])
    smB, sm0B = put("smB", rB + 16 * K, [P, 2, T]), put("sm0B", rB + 18 * K, [P, 2, P])
    wcmp = put("wcmp", rA, [P, 32, P])
    q4 = t1
    lr = put("lr", rM, [P, 4, T])
    li = put("li", rM + 4 * K, [P, 4, T])
    la = put("la", rM + 8 * K, [P, 4, T])
    lt = put("lt", rM + 12 * K, [P, 4, T])
    u_2 = put("u_2", rA, [P, 8, T])
    q_2 = put("q_2", rA + 8 * K, [P, 8, T])
    ag_2 = put("ag_2", rA + 16 * K, [P, 8, T])
    k_2 = put("k_2", rA + 24 * K, [P, 2, T])
    v_2 = put("v_2", rA + 28 * K, [P, 2, T])
    z_2 = put("z_2", rB, [P, 8, T])
    at_ = (put("at_hi", rB + 8 * K, [P, 8, T], F32R), put("at_lo", rB + 16 * K, [P, 8, T], F32R))
    gs_2 = put("gs_2", rB + 8 * K, [P, DC, T])
    y_2 = put("y_2", rA + 24 * K, [P, 8, T])
    ys = (put("ys_hi", rH, [P, 8, T], F32R), put("ys_lo", rH + 8 * K, [P, 8, T], F32R))
    sg = (put("sg_hi", rA, [P, 8, T], F32R), put("sg_lo", rA + 24 * K, [P, 8, T], F32R))
    mg2 = put("mg2", rA + 8 * K, [P, DC, T])
    kg2 = put("kg2", rM + 9 * K, [P, T])
    vg2 = put("vg2", rM + 10 * K, [P, 2, 64])
    qg2 = put("qg2", rM + 11 * K, [P, 2, T])
    sm2 = put("sm2", rM + 13 * K, [P, T])
    pt2 = put("pt2", rM + 14 * K, [P, 384])
    sm20 = put("sm20", rM + 15 * K + 512, [P, P])
    sm2B, sm20B = put("sm2B", rM, [P, T]), put("sm20B", rM + K, [P, P])
    ph = put("ph", rB + 24 * K, [P, 4, 32, 16])
    ssb = [put(f"ssb{n}", rM + 2 * K * n, [P, 2, T]) for n in range(8)]
    vec = put("vec", rS, [P, NVEC])
    off = rS + (NVEC * 4 + 63) // 64 * 64
    mod = put("mod", off, [P, 96]); off += 384
    adat = put("adat", off, [P, 4]); off += 64
    gates = put("gates", off, [P, 2, 48]); off += 384
    ones = put("ones", off, [P, P]); off += 512
    halves = put("halves", off, [P, P]); off += 512
    ident = put("ident", off, [P, P]); off += 512
    causal = put("causal", off, [P, 2, T]); off += 2048
    band = put("band", off, [P, T]); off += 1024
    cmask = put("cmask", off, [P, 2, 16]); off += 128
    cadd = put("cadd", off, [P, 2, 16]); off += 128
    rstd = put("rstd", off, [P, T]); off += 1024
    cc = put("cc", off, [P, DC, 2], F32R); off += 128
    cs = put("cs", off, [P, 2, DC]); off += 128
    scA = put("scA", off, [P, DC]); off += 64
    l8 = put("l8", off, [P, DC]); off += 64
    ltmp = put("ltmp", off, [P, 4, DC]); off += 256
    w2 = put("w2", rM, [P, 2, P])
    ssp = put("ssp", off, [P, 5, 32]); off += 640
    wgate = put("wgate", off, [P, 2, 4, P])
    bz = put("bz", off, [P, 2, P])
    cz = put("cz", off + 1024, [P, 2, 4, 32])
    cz2 = put("cz2", off + 2048, [P, 2, 4, 32])
    uc = put("uc", off + 3072, [P, T])

    def V(name, n=0, w=1):
        return vec[:, VEC[name] + n:VEC[name] + n + w]

    def Vd(name, at, w=1):
        return vec[:, bass.ds(at + VEC[name], w)]

    pairs = [ctx.enter_context(nc.psum_tensor(f"pair{n}", [P, 4, T], F32)) for n in range(2)]
    bank = [ctx.enter_context(nc.psum_tensor(f"bank{n}", [P, 2, T], F32)) for n in range(4)]

    def sem(name):
        return ctx.enter_context(nc.semaphore(name))

    w_loaded = [sem(f"w_loaded{n}") for n in range(RAW)]
    hi_ready, lo_ready, pe_units = sem("hi_ready"), sem("lo_ready"), sem("pe_units")
    evacuated, ev_used = sem("evacuated"), sem("ev_used")
    consts_in, consts_made, x_in = sem("consts_in"), sem("consts_made"), sem("x_in")
    x_back = sem("x_back")
    residual_done = sem("residual_done")
    to_act, to_pe, to_pool = sem("dve_to_act"), sem("dve_to_pe"), sem("dve_to_pool")
    act_to_dve, act_to_pe = sem("act_to_dve"), sem("act_to_pe")
    pe_to_dve, pe_to_act = sem("pe_to_dve"), sem("pe_to_act")
    pool_to_pe, pool_to_dve = sem("pool_to_pe"), sem("pool_to_dve")
    pool_dma = sem("pool_dma")
    stored = sem("stored")
    S = dict(to_act=to_act, to_pe=to_pe, to_pool=to_pool, act_to_dve=act_to_dve, act_to_pe=act_to_pe,
             pe_to_dve=pe_to_dve, pe_to_act=pe_to_act, pool_to_pe=pool_to_pe, pool_to_dve=pool_to_dve, pool_dma=pool_dma)

    X = {"h": h, "oa": oa, "ob": ob, "hid": hid, "ys": ys, "at": at_, "sg": sg}
    PH = phases()
    N_UNITS = sum(ph.units * ph.count for ph in PH)
    block = ctx.enter_context(nc.Block())

    class Tally:

        def __init__(self):
            self.n = {k: Lin({"to_pe": 1, "act_to_dve": 2, "to_pool": 1}.get(k, 0)) for k in S}

        def step(self, key, k=1):
            self.n[key] = self.n[key] + k
            return self.n[key].value()

    def grown(run):
        j, fresh = Job(None, None, Tally()), Tally()
        run(j)
        return {k: j.t.n[k].c - fresh.n[k].c for k in S}

    def repeat(j, count, run, body):
        start, grow = dict(j.t.n), grown(run)

        def once(i):
            for k in S:
                j.t.n[k] = start[k].over(i, grow[k])
            body(i)

        if count == 1:
            once(0)
        elif j.me in ("pool",) and not any(grow[k] for k in ("pool_dma", "pool_to_pe", "pool_to_dve")):
            pass
        else:
            with j.eng.Fori(0, count) as i:
                once(i)
        for k in S:
            j.t.n[k] = Lin(start[k].c + grow[k] * count)

    def whole_side(ph, d):
        for _ in woven(ph, 0, d)[0]:
            pass
        for gr in ph.groups:
            side(ph, gr, 0, d)

    def walk(me, eng, unit, group_end):
        j = Job(me, eng, Tally())
        u, g = Lin(0), Lin(0)
        for ph in PH:
            before(ph, j)
            steps = sum(1 for _ in woven(ph, 0, Job(None, None, Tally()))[0])

            def body(i, ph=ph, u=u, g=g, steps=steps):
                uu, gg = u.over(i, ph.units), g.over(i, len(ph.groups))
                job, first, last = woven(ph, i, j)
                state = [0]

                def weave(at):
                    if first < at <= last:
                        goal = (at - first) * steps // (last - first)
                        while state[0] < goal:
                            next(job)
                            state[0] += 1
                        if at == last:
                            for _ in job:
                                pass

                at = 0
                for gr in ph.groups:
                    end = at + 2 * gr.slots
                    for n in range(2 * gr.slots):
                        if me != "pe":
                            weave(at + 1)
                        unit(ph, gr, uu, gg, n, i)
                        uu = uu + 1
                        at += 1
                        if me == "pe":
                            weave(at)
                    group_end(ph, gr, uu, gg, i)
                    side(ph, gr, i, j)
                    gg = gg + 1

            repeat(j, ph.count, lambda d, ph=ph: whole_side(ph, d), body)
            u, g = u + ph.units * ph.count, g + len(ph.groups) * ph.count

    def nothing(*a):
        pass


    class Job:
        def __init__(self, me, eng, tally):
            self.me, self.eng, self.t = me, eng, tally

        def sync(self, key, frm, to, ins=None, k=1):
            v = self.t.step(key, k)
            if self.me == frm:
                ins.then_inc(S[key], k)
            if self.me == to:
                self.eng.wait_ge(S[key], v)

        def give(self, key, frm, ins):
            v = self.t.step(key)
            if self.me == frm:
                ins.then_inc(S[key], 1)
            return v

        def take(self, key, to, v):
            if self.me == to:
                self.eng.wait_ge(S[key], v)

        def hand(self, key, frm, to, ins=None):
            v = self.give(key, frm, ins)
            yield
            self.take(key, to, v)

    ve, sc, te, po = nc.vector, nc.scalar, nc.tensor, nc.gpsimd

    def split(dst, at, n, src):
        hi, lo = dst
        ve.tensor_copy(hi[:, bass.ds(at, n), :], src)
        ve.drain()
        return ve.tensor_tensor(lo[:, bass.ds(at, n), :], src, hi[:, bass.ds(at, n), :].bitcast(F32), ALU.subtract)

    def norm(j, gain_scale, gain_shift, in_place):
        me = j.me
        for c in range(0, DC, 4):
            tt = (t1, t2)[c // 4 % 2]
            ins = None
            if me == "dve":
                if c >= 8:
                    j.eng.wait_ge(pe_to_dve, sq_read[c // 4 - 2])
                ins = ve.tensor_tensor(tt[:, :, :], res[:, c:c + 4, :], res[:, c:c + 4, :], ALU.mult)
            j.sync("to_pe", "dve", "pe", ins)
            if me == "pe":
                for n in range(4):
                    ins = te.matmul(bank[0][:, 0, :], ones[:, :], tt[:, n, :], start=(c + n == 0),
                                    stop=(c + n == DC - 1))
                ins.then_inc(pe_to_dve, 1)
            v = j.t.step("pe_to_dve")
            if c == 0:
                sq_read = []
            sq_read.append(v)
        ins = None
        if me == "dve":
            j.eng.wait_ge(pe_to_dve, sq_read[-1])
            ins = ve.tensor_scalar(rstd[:, :], bank[0][:, 0, :], 1.0 / D, EPS, ALU.mult, ALU.add)
        j.sync("to_act", "dve", "act", ins)
        if me == "act":
            ins = sc.activation(rstd[:, :], rstd[:, :], ACT.Sqrt)
        j.sync("act_to_dve", "act", "dve", ins)
        if me == "dve":
            ve.reciprocal(rstd[:, :], rstd[:, :])
            if gain_shift is not None:
                ve.scalar_tensor_tensor(out=scA[:, :], in0=mod[:, gain_scale[1]:gain_scale[1] + DC], scalar=1.0,
                                        in1=V(gain_scale[0], 0, DC), op0=ALU.add, op1=ALU.mult)
            else:
                ve.tensor_copy(scA[:, :], V(gain_scale[0], 0, DC))
            ve.drain()
            for c in range(0, DC, 4):
                tt = (t1, t2)[c // 4 % 2] if not in_place else res[:, c:c + 4, :]
                rs = rstd[:, :].unsqueeze(1).broadcast_to([P, 4, T])
                ve.tensor_tensor(tt[:, :, :], res[:, c:c + 4, :], rs, ALU.mult)
                ve.drain()
                for n in range(4):
                    if gain_shift is not None:
                        ve.tensor_scalar(tt[:, n, :], tt[:, n, :], scA[:, c + n:c + n + 1],
                                         mod[:, gain_shift + c + n:gain_shift + c + n + 1], ALU.mult, ALU.add)
                    else:
                        ve.tensor_scalar(tt[:, n, :], tt[:, n, :], scA[:, c + n:c + n + 1], None, ALU.mult)
                ve.drain()
                if not in_place:
                    split(h, c, 4, tt[:, :, :])
                    ve.drain()

    def ready(j):
        ins = ve.drain() if j.me == "dve" else None
        j.sync("to_pe", "dve", "pe", ins)

    def compress(j, which):
        me = j.me
        pos = "cmp_pos_k" if which == 0 else "cmp_pos_v"
        ins = None
        if me == "pool":
            j.eng.wait_ge(to_pe, j.t.n["to_pe"].value())
            if which == 1:
                j.eng.wait_ge(pe_to_dve, COMP_PE[0])
            po.dma_start(wcmp[:, :, :], small["cmp_w1"][which].rearrange("l d e -> d l e")).then_inc(pool_dma, 16)
            po.dma_start(w2[:, which, :], small["cmp_w2"][which]).then_inc(pool_dma, 16)
        for l in range(32):
            if l % 8 == 0:
                yield
            if me == "dve":
                ve.tensor_scalar(blocks[:, l, :].rearrange("p (g n) -> p g n", g=4),
                                 kc4[:, :, l:l + 225:16], V(pos, l), None, ALU.add)
        ins = ve.drain() if me == "dve" else None
        yield from j.hand("to_pe", "dve", "pe", ins)
        v = j.t.step("pool_dma", 32)
        if me == "pe":
            j.eng.wait_ge(pool_dma, v)
            for l in range(32):
                ins = te.matmul(bank[1][:, 0, 0:60], wcmp[:, l, :], blocks[:, l, :], start=(l == 0), stop=(l == 31))
            ins.then_inc(pe_to_act, 1)
        v = j.t.step("pe_to_act")
        yield
        if me == "act":
            j.eng.wait_ge(pe_to_act, v)
            ins = sc.activation(hidc[:, which, 0:60], bank[1][:, 0, 0:60], ACT.Gelu_apprx_tanh)
        yield from j.hand("act_to_pe", "act", "pe", ins)
        if me == "pe":
            if which == 0:
                ins = te.matmul(bank[2][:, 0, 0:60], w2[:, 0, :], hidc[:, 0, 0:60], start=True, stop=True)
            else:
                for g in range(4):
                    ins = te.matmul(bank[2][0:N_CMP, :, :].rearrange("p a b -> p (a b)")[:, g * P:(g + 1) * P],
                                    hidc[:, 1, g * N_CMP:(g + 1) * N_CMP], w2[:, 1, :], start=True, stop=True)
            ins.then_inc(pe_to_dve, 1)
        v = j.t.step("pe_to_dve")
        COMP_PE[which] = v
        yield
        if me == "dve":
            j.eng.wait_ge(pe_to_dve, v)
            if which == 0:
                ve.tensor_copy(kcmp[:, 0:60], bank[2][:, 0, 0:60])
            else:
                ve.tensor_copy(vcmp[0:N_CMP, :, :].rearrange("p a b -> p (a b)"),
                               bank[2][0:N_CMP, :, :].rearrange("p a b -> p (a b)"))
            ve.drain()

    COMP_PE = {}

    def nsa(j, i):
        me = j.me
        SCALE = float(P) ** -0.5
        ins = None
        if me == "dve":
            ins = ve.drain()
        yield from j.hand("to_pool", "dve", "pool", ins)
        if me == "pool":
            po.tensor_copy(kg[:, :, :], k2[:, :, bass.ds(i, 1), :].rearrange("p a o t -> p a (o t)"))
            for br in range(2):
                po.tensor_copy(vg[:, br, :, :], v2[:, br, :, bass.ts(i, P)])
            po.tensor_copy(kcg[:, 0:N_CMP], kcmp[:, bass.ts(i, N_CMP)])
            po.tensor_copy(vcg[0:N_CMP, :], vcmp[0:N_CMP, bass.ds(i, 1), :].rearrange("p o d -> p (o d)"))
            ins = po.drain()
        yield from j.hand("pool_to_pe", "pool", "pe", ins)
        if me == "pe":
            for b in range(2):
                for hd in range(4):
                    ins = te.matmul(bank[3][:, b, 16 * hd:16 * hd + N_CMP], q4[:, hd, b * P:(b + 1) * P],
                                    kcg[:, 0:N_CMP], start=True, stop=True)
        yield from j.hand("pe_to_dve", "pe", "dve", ins)
        sv = pc[:, :, 0:N_CMP]
        sv4 = pc[:, :, :].rearrange("p (b h) n -> p b h n", b=2)[:, :, :, 0:N_CMP]
        if me == "dve":
            src = bank[3][:, :, 0:64].rearrange("p b (h n) -> p b h n", h=4)[:, :, :, 0:N_CMP]
            for b in range(2):
                ve.scalar_tensor_tensor(out=sv4[:, b], in0=src[:, b], scalar=SCALE,
                                        in1=cadd[:, b, 0:N_CMP].unsqueeze(1).broadcast_to([P, 4, N_CMP]),
                                        op0=ALU.mult, op1=ALU.add)
            ve.drain()
            ve.tensor_reduce(st[:, 0:8], sv, AX.X, ALU.max)
            ve.drain()
            ve.tensor_tensor(sv, sv, st[:, 0:8].unsqueeze(2).broadcast_to([P, 8, N_CMP]), ALU.subtract)
            ins = ve.drain()
        yield from j.hand("to_act", "dve", "act", ins)
        if me == "act":
            ins = sc.activation(sv, sv, ACT.Exp)
        yield from j.hand("act_to_dve", "act", "dve", ins)
        if me == "dve":
            for b in range(2):
                ve.tensor_tensor(sv4[:, b], sv4[:, b], cmask[:, b, 0:N_CMP].unsqueeze(1).broadcast_to([P, 4, N_CMP]),
                                 ALU.mult)
            ve.drain()
            ve.tensor_reduce(st[:, 8:16], sv, AX.X, ALU.add)
            ve.drain()
            ve.tensor_scalar(st[:, 16:24], st[:, 8:16], 1e-30, None, ALU.max)
            ve.drain()
            ve.reciprocal(st[:, 24:32], st[:, 16:24])
            ve.drain()
            by_b = lambda at, hd: st[:, at:at + 8].rearrange("p (b h) -> p b h", b=2)[:, :, hd:hd + 1]
            for hd in range(4):
                ve.tensor_tensor(by_b(32, hd), by_b(24, hd), gates[:, :, bass.ds(i * 12 + 3 * hd, 1)], ALU.mult)
            ve.drain()
            ins = ve.tensor_tensor(sv, sv, st[:, 32:40].unsqueeze(2).broadcast_to([P, 8, N_CMP]), ALU.mult)
        yield from j.hand("to_pe", "dve", "pe", ins)
        if me == "pe":
            for b in range(2):
                for hd in range(4):
                    ins = te.transpose(bank[1 + hd // 2][0:N_CMP, hd % 2, b * P:(b + 1) * P],
                                       pc[:, 4 * b + hd, 0:N_CMP], ident[:, :])
        yield from j.hand("pe_to_act", "pe", "act", ins)
        if me == "act":
            for hd2 in range(2):
                ins = sc.activation(pct[0:N_CMP, 2 * hd2:2 * hd2 + 2, :], bank[1 + hd2][0:N_CMP, :, :], ACT.Copy)
        yield from j.hand("act_to_pe", "act", "pe", ins)
        buf = lambda hd: ((sm0, sm), (sm0B, smB))[hd % 2]

        def scores(hd):
            for br in range(2):
                te.matmul(bank[3][:, 1, br * P:(br + 1) * P], q4[:, hd, 0:P], kg[:, br, 0:P], start=True, stop=True)
            for br in range(2):
                ins = te.matmul(bank[0][:, br, :], q4[:, hd, P:T], kg[:, br, :], start=True, stop=True)
            return ins

        def shift(hd):
            s0, s1 = buf(hd)
            for b, s_in, s_out in ((0, bank[3][:, 1, :].rearrange("p (r t) -> p r t", r=2), s0),
                                   (1, bank[0][:, :, :], s1)):
                w = P * (b + 1)
                ve.scalar_tensor_tensor(out=s_out[:, :, :], in0=s_in, scalar=SCALE,
                                        in1=causal[:, b, 0:w].unsqueeze(1).broadcast_to([P, 2, w]),
                                        op0=ALU.mult, op1=ALU.add)
            ve.drain()
            ve.tensor_reduce(st[:, 40:42], s0[:, :, :], AX.X, ALU.max)
            ve.tensor_reduce(st[:, 42:44], s1[:, :, :], AX.X, ALU.max)
            ve.drain()
            return ve.tensor_scalar(st[:, 44:48], st[:, 40:44], -1.0, None, ALU.mult)

        def exponentials(hd):
            for b in range(2):
                for br in range(2):
                    c, x = 2 * b + br, buf(hd)[b]
                    ins = sc.activation(x[:, br, :], x[:, br, :], ACT.Exp, bias=st[:, 44 + c:45 + c],
                                        accum_out=st[:, 48 + c:49 + c])
            return ins

        def weights(hd):
            ve.reciprocal(st[:, 52:56], st[:, 48:52])
            ve.drain()
            by_br = lambda at: st[:, at:at + 4].rearrange("p (b r) -> p b r", b=2)
            ve.tensor_tensor(by_br(56), by_br(52), gates[:, :, bass.ds(i * 12 + 3 * hd + 1, 2)], ALU.mult)
            ve.drain()
            for b in range(2):
                for br in range(2):
                    c, x = 2 * b + br, buf(hd)[b]
                    ins = ve.tensor_scalar(x[:, br, :], x[:, br, :], st[:, 56 + c:57 + c], None, ALU.mult)
            return ins

        ins = scores(0) if me == "pe" else None
        yield from j.hand("pe_to_dve", "pe", "dve", ins)
        ins = shift(0) if me == "dve" else None
        shifted = j.give("to_act", "dve", ins)
        scores_used = j.give("to_pe", "dve", ve.drain() if me == "dve" else None)
        yield
        j.take("to_act", "act", shifted)
        ins = exponentials(0) if me == "act" else None
        exp_done = j.give("act_to_dve", "act", ins)
        j.take("to_pe", "pe", scores_used)
        ins = scores(1) if me == "pe" else None
        scored = j.give("pe_to_dve", "pe", ins)
        yield
        for hd in range(4):
            j.take("act_to_dve", "dve", exp_done)
            ins = weights(hd) if me == "dve" else None
            weighted = j.give("to_pe", "dve", ins)
            if hd == 0:
                j.take("pe_to_dve", "dve", scored)
            if hd < 3:
                ins = shift(hd + 1) if me == "dve" else None
                shifted = j.give("to_act", "dve", ins)
                scores_used = j.give("to_pe", "dve", ve.drain() if me == "dve" else None)
            yield
            j.take("to_pe", "pe", weighted)
            if me == "pe":
                s0, s1 = buf(hd)
                for br in range(2):
                    flat = bank[1 + br][:, :, :].rearrange("p a b -> p (a b)")
                    te.transpose(flat[:, 0:P], s0[:, br, :], ident[:, :])
                    for m in range(2):
                        ins = te.transpose(flat[:, (m + 1) * P:(m + 2) * P], s1[:, br, m * P:(m + 1) * P], ident[:, :])
            yield from j.hand("pe_to_act", "pe", "act", ins)
            if me == "act":
                for br in range(2):
                    ins = sc.activation(pt[:, br, :], bank[1 + br][:, :, :].rearrange("p a b -> p (a b)")[:, 0:384],
                                        ACT.Copy)
            copied = j.give("act_to_pe", "act", ins)
            if hd < 3:
                j.take("to_act", "act", shifted)
                ins = exponentials(hd + 1) if me == "act" else None
                exp_done = j.give("act_to_dve", "act", ins)
            yield
            j.take("act_to_pe", "pe", copied)
            if hd < 3:
                j.take("to_pe", "pe", scores_used)
            if me == "pe":
                te.matmul(bank[3][:, 0, :], vcg[0:N_CMP, :], pct[0:N_CMP, hd, :], start=True, stop=False,
                          skip_group_check=True)
                for br in range(2):
                    te.matmul(bank[3][:, 0, :], vg[:, br, 0, :], pt[:, br, 0:T], start=False, stop=False,
                              skip_group_check=True)
                    ins = te.matmul(bank[3][:, 0, P:T], vg[:, br, 1, :], pt[:, br, T:384], start=False,
                                    stop=(br == 1), skip_group_check=True)
                if hd < 2:
                    ins = scores(hd + 2)
            yield from j.hand("pe_to_dve", "pe", "dve", ins)
            if me == "dve":
                split(oa, i * 4 + hd, 1, bank[3][:, 0:1, :])
                ve.drain()

    def conv(dst, src, taps, wname, bname, ci, stride):
        for n in range(4):
            ve.tensor_scalar(dst[:, n, :], src[:, n, :], Vd(wname, ci + ((taps - 1) * stride + n)),
                             Vd(bname, ci + n), ALU.mult, ALU.add)
        for s in range(1, taps):
            ve.drain()
            for n in range(4):
                last = ve.scalar_tensor_tensor(out=dst[:, n, s:T], in0=src[:, n, 0:T - s],
                                               scalar=Vd(wname, ci + ((taps - 1 - s) * stride + n)),
                                               in1=dst[:, n, s:T], op0=ALU.mult, op1=ALU.add)
        return last

    def lru(j, i):
        me = j.me
        ins = None
        if me == "dve":
            ins = ve.drain()
        yield from j.hand("to_pe", "dve", "pe", ins)
        if me == "pool":
            j.eng.wait_ge(to_pe, j.t.n["to_pe"].value())
            po.dma_start(wgate[:, 0, :, :], small["lru_wa"][bass.ts(i, 4)].rearrange("c d e -> d c e")).then_inc(pool_dma, 16)
            po.dma_start(wgate[:, 1, :, :], small["lru_wi"][bass.ts(i, 4)].rearrange("c d e -> d c e")).then_inc(pool_dma, 16)
        v = j.t.step("pool_dma", 32)
        if me == "pe":
            j.eng.wait_ge(pool_dma, v)
            for a in range(2):
                for n in range(4):
                    ins = te.matmul(bank[2 * a + n // 2][:, n % 2, :], wgate[:, a, n, :], t1[:, n, :],
                                    start=True, stop=True)
        yield from j.hand("pe_to_act", "pe", "act", ins)
        for a, dst, bname in ((0, lr, "lru_ba"), (1, li, "lru_bi")):
            if me == "act":
                for n in range(4):
                    ins = sc.activation(dst[:, n, :], bank[2 * a + n // 2][:, n % 2, :], ACT.Sigmoid,
                                        bias=Vd(bname, i * 4 + n))
            yield
        if me == "act":
            sc.drain()
            for n in range(4):
                sc.activation(lt[:, n, :], lr[:, n, :], ACT.Tanh, scale=l8[:, bass.ds(i * 4 + n, 1)])
        yield
        if me == "act":
            for n in range(4):
                ins = sc.activation(la[:, n, :], lr[:, n, :], ACT.Exp, scale=l8[:, bass.ds(i * 4 + n, 1)])
        yield from j.hand("act_to_dve", "act", "dve", ins)
        if me == "dve":
            ve.tensor_tensor(li[:, :, :], li[:, :, :], t1[:, :, :], ALU.mult)
            ve.tensor_tensor(lr[:, :, :], la[:, :, :], la[:, :, :], ALU.mult)
            ve.drain()
            ins = ve.scalar_tensor_tensor(out=lt[:, :, :].rearrange("p a b -> p (a b)"),
                                          in0=lr[:, :, :].rearrange("p a b -> p (a b)"), scalar=1.0,
                                          in1=lt[:, :, :].rearrange("p a b -> p (a b)"), op0=ALU.add, op1=ALU.mult)
        yield from j.hand("to_act", "dve", "act", ins)
        if me == "act":
            ins = sc.activation(lt[:, :, :], lt[:, :, :], ACT.Sqrt, scale=-1.0)
        yield from j.hand("act_to_dve", "act", "dve", ins)
        if me == "dve":
            ve.tensor_tensor(li[:, :, :], li[:, :, :], lt[:, :, :], ALU.mult)
            ve.drain()
        yield
        if me == "dve":
            for n in range(4):
                ve.tensor_tensor_scan(out=lr[:, n, :], data0=la[:, n, :], data1=li[:, n, :], initial=0.0,
                                      op0=ALU.mult, op1=ALU.add)
            ve.drain()
        yield
        if me == "dve":
            ve.tensor_tensor(lr[:, :, :], lr[:, :, :], t2[:, :, :], ALU.mult)
            ve.drain()
            split(ob, i * 4, 4, lr[:, :, :])
            ve.drain()

    def head_norm(j, src, n):
        me = j.me
        ins = ve.tensor_tensor(t1[:, 0:n, :], src, src, ALU.mult) if me == "dve" else None
        j.sync("to_pe", "dve", "pe", ins)
        if me == "pe":
            for c in range(n):
                ins = te.matmul(bank[c // 2][:, c % 2, :], halves[:, :], t1[:, c, :], start=True, stop=True)
        j.sync("pe_to_dve", "pe", "dve", ins)
        if me == "dve":
            for c in range(0, n, 2):
                ve.tensor_scalar(t2[:, c:c + 2, :], bank[c // 2][:, :, :], 1.0 / 64, EPS, ALU.mult, ALU.add)
            ins = ve.drain()
        j.sync("to_act", "dve", "act", ins)
        if me == "act":
            ins = sc.activation(t2[:, 0:n, :], t2[:, 0:n, :], ACT.Sqrt)
        j.sync("act_to_dve", "act", "dve", ins)
        if me == "dve":
            ve.reciprocal(t2[:, 0:n, :], t2[:, 0:n, :])
            ve.drain()
            ve.tensor_tensor(t2[:, 0:n, :], src, t2[:, 0:n, :], ALU.mult)
            ve.drain()

    def attention2_pair(j, pair):
        for e in range(2):
            yield from attention2(j, pair, e)

    def attention2(j, pair, e):
        me = j.me
        ins, g = None, pair * 2 + e
        if me == "dve":
            for half in range(2):
                ve.tensor_copy(kg2[64 * half:64 * half + 64, :].unsqueeze(1),
                               k_2[64 * e:64 * e + 64, bass.ds(pair, 1), :])
            ins = ve.drain()
        yield from j.hand("to_pool", "dve", "pool", ins)
        if me == "pool":
            po.tensor_copy(vg2[:, :, :], v_2[:, :, bass.ts(g, 64)])
            po.tensor_copy(qg2[:, :, :], q_2[:, bass.ts(g, 2), :])
            ins = po.drain()
        yield from j.hand("pool_to_pe", "pool", "pe", ins)
        rows = lambda hd: slice(64 * (hd % 2), 64 * (hd % 2) + 64)

        def scores(hd):
            r = rows(hd)
            te.matmul(bank[0][:, 1, 0:P], qg2[r, hd // 2, 0:P], kg2[r, 0:P], start=True, stop=True)
            return te.matmul(bank[0][:, 0, :], qg2[r, hd // 2, P:T], kg2[r, :], start=True, stop=True)

        buf = lambda hd: ((sm20, sm2), (sm20B, sm2B))[hd % 2]

        def shift(hd):
            s0, s1 = buf(hd)
            sink = Vd("sinks", g * 4 + hd).broadcast_to([P, 2])
            ve.scalar_tensor_tensor(out=s0[:, :], in0=bank[0][:, 1, 0:P], scalar=0.125, in1=causal[:, 0, 0:P],
                                    op0=ALU.mult, op1=ALU.add)
            ve.scalar_tensor_tensor(out=s1[:, :], in0=bank[0][:, 0, :], scalar=0.125, in1=band[:, :],
                                    op0=ALU.mult, op1=ALU.add)
            ve.drain()
            ve.tensor_reduce(st2[:, 0:1], s0[:, :], AX.X, ALU.max)
            ve.tensor_reduce(st2[:, 1:2], s1[:, :], AX.X, ALU.max)
            ve.drain()
            ve.tensor_tensor(st2[:, 2:4], st2[:, 0:2], sink, ALU.max)
            ve.drain()
            ve.tensor_scalar(st2[:, 4:6], st2[:, 2:4], -1.0, None, ALU.mult)
            return ve.tensor_tensor(st2[:, 6:8], sink, st2[:, 2:4], ALU.subtract)

        def exponentials(hd):
            s0, s1 = buf(hd)
            sc.activation(st2[:, 8:10], st2[:, 6:8], ACT.Exp)
            sc.activation(s0[:, :], s0[:, :], ACT.Exp, bias=st2[:, 4:5], accum_out=st2[:, 10:11])
            return sc.activation(s1[:, :], s1[:, :], ACT.Exp, bias=st2[:, 5:6], accum_out=st2[:, 11:12])

        def weights(hd):
            s0, s1 = buf(hd)
            ve.tensor_tensor(st2[:, 12:14], st2[:, 8:10], st2[:, 10:12], ALU.add)
            ve.drain()
            ve.reciprocal(st2[:, 14:16], st2[:, 12:14])
            ve.drain()
            ve.tensor_scalar(s0[:, :], s0[:, :], st2[:, 14:15], None, ALU.mult)
            return ve.tensor_scalar(s1[:, :], s1[:, :], st2[:, 15:16], None, ALU.mult)

        ins = scores(0) if me == "pe" else None
        yield from j.hand("pe_to_dve", "pe", "dve", ins)
        ins = shift(0) if me == "dve" else None
        shifted = j.give("to_act", "dve", ins)
        scores_used = j.give("to_pe", "dve", ve.drain() if me == "dve" else None)
        yield
        j.take("to_act", "act", shifted)
        ins = exponentials(0) if me == "act" else None
        exp_done = j.give("act_to_dve", "act", ins)
        j.take("to_pe", "pe", scores_used)
        ins = scores(1) if me == "pe" else None
        scored = j.give("pe_to_dve", "pe", ins)
        yield
        for hd in range(4):
            r = rows(hd)
            j.take("act_to_dve", "dve", exp_done)
            ins = weights(hd) if me == "dve" else None
            weighted = j.give("to_pe", "dve", ins)
            if hd == 0:
                j.take("pe_to_dve", "dve", scored)
            if hd < 3:
                ins = shift(hd + 1) if me == "dve" else None
                shifted = j.give("to_act", "dve", ins)
                scores_used = j.give("to_pe", "dve", ve.drain() if me == "dve" else None)
            yield
            j.take("to_pe", "pe", weighted)
            if me == "pe":
                s0, s1 = buf(hd)
                flat = bank[1][:, :, :].rearrange("p a b -> p (a b)")
                te.transpose(flat[:, 0:P], s0[:, :], ident[:, :])
                for m in range(2):
                    ins = te.transpose(flat[:, (m + 1) * P:(m + 2) * P], s1[:, m * P:(m + 1) * P], ident[:, :])
            yield from j.hand("pe_to_act", "pe", "act", ins)
            if me == "act":
                ins = sc.activation(pt2[:, :], bank[1][:, :, :].rearrange("p a b -> p (a b)")[:, 0:384], ACT.Copy)
            copied = j.give("act_to_pe", "act", ins)
            if hd < 3:
                j.take("to_act", "act", shifted)
                ins = exponentials(hd + 1) if me == "act" else None
                exp_done = j.give("act_to_dve", "act", ins)
            yield
            j.take("act_to_pe", "pe", copied)
            if hd < 3:
                j.take("to_pe", "pe", scores_used)
            if me == "pe":
                te.matmul(bank[3][r, 0, :], vg2[:, 0, :], pt2[:, 0:T], start=True, stop=False, skip_group_check=True)
                ins = te.matmul(bank[3][r, 0, P:T], vg2[:, 1, :], pt2[:, T:384], start=False, stop=True,
                                skip_group_check=True)
                if hd < 2:
                    ins = scores(hd + 2)
            yield from j.hand("pe_to_dve", "pe", "dve", ins)
            if hd % 2 and me == "dve":
                ve.tensor_tensor(t1[:, 0:1, :], bank[3][:, 0:1, :], ag_2[:, bass.ds(g * 2 + hd // 2, 1), :], ALU.mult)
                ve.drain()
                split(at_, g * 2 + hd // 2, 1, t1[:, 0:1, :])
                ve.drain()

    st2 = ltmp[:, 0, :]
    MAG, CFR, CFI, W1, W2 = (ssp[:, n, :] for n in range(5))

    def cmul(o_re, o_im, a_re, a_im, b_re, b_im, x, y, conj=False, on=None):
        en = on or ve
        en.tensor_tensor(x, a_re, b_re, ALU.mult)
        en.tensor_tensor(y, a_im, b_im, ALU.mult)
        en.drain()
        en.tensor_tensor(o_re, x, y, ALU.add if conj else ALU.subtract)
        en.drain()
        en.tensor_tensor(x, a_re, b_im, ALU.mult)
        en.tensor_tensor(y, a_im, b_re, ALU.mult)
        en.drain()
        last = en.tensor_tensor(o_im, x, y, ALU.subtract if conj else ALU.add)
        en.drain()
        return last

    def spill(j):
        j.sync("to_pool", "dve", "pool", ve.drain() if j.me == "dve" else None)
        if j.me == "pool":
            po.dma_start(outT.rearrange("(c p) t -> p c t", p=P), res[:, :, :]).then_inc(pool_dma, 16)
        j.t.step("pool_dma", 16)

    def ssm_tables(j):
        me = j.me
        dt_, th, rr, s1, c1, x, y = (ssb[n][:, a, 0:32] for n, a in ((0, 0), (0, 1), (1, 0), (1, 1), (2, 0), (2, 1), (3, 0)))
        ins = None
        spill(j)
        for _ in range(8):
            yield
        if me == "dve":
            j.eng.wait_ge(pool_dma, j.t.n["pool_dma"].value())
            ins = ve.drain()
        yield from j.hand("to_act", "dve", "act", ins)
        if me == "act":
            ins = sc.activation(dt_, V("log_dt", 0, 32), ACT.Exp)
        yield from j.hand("act_to_dve", "act", "dve", ins)
        if me == "dve":
            ve.tensor_tensor(th, dt_, V("A_im", 0, 32), ALU.mult)
            ve.tensor_tensor(x, dt_, V("A_re", 0, 32), ALU.mult)
            ve.drain()
            magic = 12582912.0
            two_pi = 6.283185307179586
            p1 = 6.28125
            p2 = 0.0019350051879882812
            p3 = two_pi - p1 - p2
            ve.tensor_scalar(y, th, 1.0 / two_pi, None, ALU.mult)
            ve.drain()
            ve.tensor_scalar(y, y, magic, None, ALU.add)
            ve.drain()
            ve.tensor_scalar(y, y, -magic, None, ALU.add)
            ve.drain()
            ve.tensor_copy(rr, th)
            ve.drain()
            for part in (p1, p2, p3):
                ve.scalar_tensor_tensor(out=rr, in0=y, scalar=-part, in1=rr, op0=ALU.mult, op1=ALU.add)
                ve.drain()
            ve.tensor_scalar(rr, rr, 0.5, None, ALU.mult)
            ve.drain()
            ins = ve.tensor_scalar(c1, rr, -1.0, two_pi / 4, ALU.mult, ALU.add)
            ve.drain()
            ve.tensor_scalar(rr, rr, -3.1415925, 3.1415925, ALU.max, ALU.min)
            ins = ve.tensor_scalar(c1, c1, -3.1415925, 3.1415925, ALU.max, ALU.min)
            ins = ve.drain()
        yield from j.hand("to_act", "dve", "act", ins)
        if me == "act":
            sc.activation(MAG, x, ACT.Exp)
            sc.activation(s1, rr, ACT.Sin)
            ins = sc.activation(W2, c1, ACT.Sin)
        yield from j.hand("act_to_dve", "act", "dve", ins)
        if me == "dve":
            ve.tensor_tensor(x, s1, W2, ALU.mult)
            ve.tensor_tensor(y, s1, s1, ALU.mult)
            ve.drain()
            ve.tensor_scalar(s1, x, 2.0, None, ALU.mult)
            ve.tensor_scalar(c1, y, -2.0, 1.0, ALU.mult, ALU.add)
            ve.drain()
            ve.tensor_tensor(x, MAG, c1, ALU.mult)
            ve.tensor_tensor(dt_, MAG, s1, ALU.mult)
            ve.tensor_tensor(th, V("A_re", 0, 32), V("A_re", 0, 32), ALU.mult)
            ve.tensor_tensor(rr, V("A_im", 0, 32), V("A_im", 0, 32), ALU.mult)
            ve.drain()
            ve.tensor_scalar(x, x, -1.0, None, ALU.add)
            ve.tensor_tensor(th, th, rr, ALU.add)
            ve.drain()
            ve.reciprocal(th, th)
            ve.drain()
            cmul(CFR, CFI, V("A_re", 0, 32), V("A_im", 0, 32), x, dt_, W1, W2, conj=True)
            ve.tensor_tensor(CFR, CFR, th, ALU.mult)
            ve.tensor_tensor(CFI, CFI, th, ALU.mult)
            ve.drain()
        er, ei, e2r, e2i = c1, s1, dt_, th
        wx = ssb[3][:, 1, :]
        wy = ssb[4][:, 0, :]
        for half in range(2):
            re, im = ph[:, 2 * half, :, :], ph[:, 2 * half + 1, :, :]
            if me == "dve":
                ve.memset(re[:, :, 0:1], 1.0)
                ve.memset(im[:, :, 0:1], 0.0)
                ve.drain()
            L = 1
            while L < 16:
                br = er.unsqueeze(2).broadcast_to([P, 32, L])
                bi = ei.unsqueeze(2).broadcast_to([P, 32, L])
                wxl = wx[:, 0:32 * L].rearrange("p (a b) -> p a b", b=L)
                wyl = wy[:, 0:32 * L].rearrange("p (a b) -> p a b", b=L)
                yield
                if me == "dve":
                    cmul(re[:, :, L:2 * L], im[:, :, L:2 * L], re[:, :, 0:L], im[:, :, 0:L], br, bi, wxl, wyl)
                    cmul(e2r, e2i, er, ei, er, ei, wx[:, 0:32], wy[:, 0:32])
                er, ei, e2r, e2i = e2r, e2i, er, ei
                L *= 2

    def load_ssm(j, m):
        if j.me == "pool":
            po.dma_start(bz[:, :, :], small["B"][bass.ds(m, 1)].rearrange("o p c s -> p (o c) s")).then_inc(pool_dma, 16)
            po.dma_start(cz[:, :, :, :], small["C"][bass.ds(m, 1)].rearrange("o p c q k -> p (o c) q k")).then_inc(pool_dma, 16)
        j.t.step("pool_dma", 32)

    def ssm(j, m):
        me = j.me
        ins = None
        loaded = j.t.n["pool_dma"].value()
        if me == "pool":
            po.tensor_copy(uc[:, :].unsqueeze(1), u_2[:, bass.ds(m, 1), :])
            ins = po.drain()
        j.sync("pool_to_pe", "pool", "pe", ins)
        f4 = lambda t: t.rearrange("p q (a b) -> p q a b", b=16)
        E = ((ssb[0][:, :, :], ssb[1][:, :, :]), (t2[:, 0:2, :], t2[:, 2:4, :]))
        phases_made = []
        for q2 in range(2):
            if me == "pool":
                j.eng.wait_ge(to_pool, j.t.n["to_pool"].value(1, q2 - 1))
                hi_ = lambda k: ph[:, 2 + k, bass.ds(m * 4 + 2 * q2, 2), :].unsqueeze(3).broadcast_to([P, 2, 16, 16])
                lo_ = lambda k: ph[:, k, bass.ds(m * 4 + 2 * q2, 2), :].unsqueeze(2).broadcast_to([P, 2, 16, 16])
                ins = cmul(f4(E[q2][0]), f4(E[q2][1]), hi_(0), hi_(1), lo_(0), lo_(1), f4(t1[:, 0:2, :]),
                           f4(t1[:, 2:4, :]), on=po)
            phases_made.append(j.give("pool_to_dve", "pool", ins))
        if me == "pe":
            j.eng.wait_ge(pool_dma, loaded)
            for q in range(4):
                for c in range(2):
                    ins = te.matmul(bank[q][:, c, :], bz[32 * q:32 * q + 32, c, :], uc[32 * q:32 * q + 32, :],
                                    start=True, stop=True)
        yield from j.hand("pe_to_act", "pe", "act", ins)
        if me == "dve":
            j.eng.wait_ge(pool_dma, loaded)
            cr = CFR[:, bass.ts(m, 4)].unsqueeze(2).broadcast_to([P, 4, 32])
            ci = CFI[:, bass.ts(m, 4)].unsqueeze(2).broadcast_to([P, 4, 32])
            x = ssb[6][:, 0, 0:128].rearrange("p (a b) -> p a b", b=32)
            y = ssb[6][:, 1, 0:128].rearrange("p (a b) -> p a b", b=32)
            cmul(cz2[:, 0, :, :], cz2[:, 1, :, :], cz[:, 0, :, :], cz[:, 1, :, :], cr, ci, x, y)
            ve.tensor_scalar(cz2[:, 1, :, :], cz2[:, 1, :, :], -1.0, None, ALU.mult)
            ve.drain()
        yield
        for q2 in range(2):
            er, ei = E[q2]
            br_, bi_ = ssb[2], ssb[3]
            x, y = ssb[6], ssb[7]
            wr, wi = ssb[4], ssb[5]
            if me == "act":
                for n in range(2):
                    sc.activation(br_[:, n, :], bank[2 * q2 + n][:, 0, :], ACT.Copy)
                    ins = sc.activation(bi_[:, n, :], bank[2 * q2 + n][:, 1, :], ACT.Copy)
            yield from j.hand("act_to_dve", "act", "dve", ins)
            j.take("pool_to_dve", "dve", phases_made[q2])
            a3 = lambda t: t[:, :, :]
            if me == "dve":
                cmul(a3(wr), a3(wi), a3(er), a3(ei), a3(br_), a3(bi_), a3(x), a3(y), conj=True)
            if q2 == 0:
                j.sync("to_pool", "dve", "pool", ve.drain() if me == "dve" else None)
                load_ssm(j, m + 1)
            yield
            if me == "dve":
                for n in range(2):
                    mg = MAG[:, bass.ds(m * 4 + 2 * q2 + n, 1)].broadcast_to([P, T])
                    ve.tensor_tensor_scan(out=br_[:, n, :], data0=mg, data1=wr[:, n, :], initial=0.0,
                                          op0=ALU.mult, op1=ALU.add)
                    ve.tensor_tensor_scan(out=bi_[:, n, :], data0=mg, data1=wi[:, n, :], initial=0.0,
                                          op0=ALU.mult, op1=ALU.add)
                ve.drain()
            yield
            if me == "dve":
                cmul(a3(wr), a3(wi), a3(er), a3(ei), a3(br_), a3(bi_), a3(x), a3(y))
                ins = ve.drain()
            j.give("to_pool", "dve", ve.drain() if me == "dve" else None)
            yield from j.hand("to_pe", "dve", "pe", ins)
            ins = ve.drain() if me == "dve" else None
            yield from j.hand("to_act", "dve", "act", ins)
            if me == "pe":
                for n in range(2):
                    q = 2 * q2 + n
                    te.matmul(bank[0][32 * q:32 * q + 32, 0, :], cz2[:, 0, q, :], wr[:, n, :], start=True,
                              stop=False, skip_group_check=True)
                    ins = te.matmul(bank[0][32 * q:32 * q + 32, 0, :], cz2[:, 1, q, :], wi[:, n, :], start=False,
                                    stop=True, skip_group_check=True)
            yield from j.hand("pe_to_dve", "pe", "dve", ins)
        if me == "dve":
            ins = ve.scalar_tensor_tensor(out=ssb[6][:, 0, :], in0=u_2[:, bass.ds(m, 1), :].rearrange("p o t -> p (o t)"),
                                          scalar=Vd("D_skip", m),
                                          in1=bank[0][:, 0, :], op0=ALU.mult, op1=ALU.add)
        for_act = j.give("to_act", "dve", ins)
        for_pe = j.give("to_pe", "dve", ve.drain() if me == "dve" else None)
        yield
        j.take("to_act", "act", for_act)
        j.take("to_pe", "pe", for_pe)
        if me == "act":
            ins = sc.activation(y_2[:, bass.ds(m, 1), :], ssb[6][:, 0:1, :], ACT.Gelu_apprx_tanh)
        yield from j.hand("act_to_dve", "act", "dve", ins)

    def before(ph, j):
        me, eng = j.me, j.eng
        if ph.name == "cmp":
            norm(j, ("norm1_g", 16), 0, False)
            if me == "dve":
                log_decay()
            ready(j)
        elif ph.name == "merge":
            ready(j)
        elif ph.name == "out":
            if me == "dve":
                for c in range(0, DC, 4):
                    split(h, c, 4, res[:, c:c + 4, :])
            ready(j)
            if me == "pool":
                eng.wait_ge(to_pe, j.t.n["to_pe"].value())
                po.dma_start(res[:, :, :], xT.rearrange("(c p) t -> p c t", p=P)).then_inc(x_back, 16)
            if me == "dve":
                eng.wait_ge(x_back, 16)
        elif ph.name == "up0":
            norm(j, ("norm2_g", 64), 48, False)
            ready(j)
        elif ph.name in ("down0", "down1", "attn_out", "ssm_out"):
            ready(j)
            if ph.name == "attn_out":
                if me == "pool":
                    eng.wait_ge(to_pe, j.t.n["to_pe"].value())
                load_ssm(j, 0)
        elif ph.name == "kv2":
            norm(j, ("final_g", 0), None, True)
            norm(j, ("norm_w_2", 0), None, False)
            ready(j)
        elif ph.name == "glu":
            j.sync("to_pool", "dve", "pool", ve.drain() if me == "dve" else None)
            if me == "pool":
                po.dma_start(res[:, :, :], outT.rearrange("(c p) t -> p c t", p=P)).then_inc(pool_dma, 16)
            j.t.step("pool_dma", 16)
            if me == "dve":
                split(ys, 0, 4, y_2[:, 0:4, :])
                split(ys, 4, 4, y_2[:, 4:8, :])
            ready(j)
        elif ph.name == "out2a":
            if me == "dve":
                for c in range(0, DC, 4):
                    split(h, c, 4, mg2[:, c:c + 4, :])
            ready(j)
            if me == "dve":
                eng.wait_ge(pool_dma, j.t.n["pool_dma"].value())

    def woven(ph, i, j):
        if ph.name == "cmp":
            return compress(j, 0), 8, 16
        if ph.name == "q0":
            return compress(j, 1), 0, 8
        if ph.name in ("nsa", "nsa3"):
            return nsa(j, 3 if ph.name == "nsa3" else i), 0, ph.units
        if ph.name == "lru":
            return lru(j, i), 16, 32
        if ph.name == "kv2":
            return ssm_tables(j), 0, 16
        if ph.name == "uz":
            return attention2_pair(j, i), 0, 16
        if ph.name == "attn_out":
            return chain(ssm(j, i * 2), ssm(j, i * 2 + 1)), 0, 24
        if ph.name == "gs":
            return chain(ssm(j, i * 2 + 4), ssm(j, i * 2 + 5)), 0, 16
        return iter(()), 0, 0

    def log_decay():
        z, s, s2, acc = ltmp[:, 3, :], ltmp[:, 0, :], ltmp[:, 1, :], ltmp[:, 2, :]
        ve.tensor_scalar(s2, z, 2.0, None, ALU.add)
        ve.drain()
        ve.reciprocal(s2, s2)
        ve.drain()
        ve.tensor_tensor(s, z, s2, ALU.mult)
        ve.drain()
        ve.tensor_tensor(s2, s, s, ALU.mult)
        ve.memset(acc, 1.0 / 19)
        ve.drain()
        for n in range(17, 0, -2):
            ve.tensor_tensor(acc, acc, s2, ALU.mult)
            ve.drain()
            ve.tensor_scalar(acc, acc, 1.0 / n, None, ALU.add)
            ve.drain()
        ve.tensor_tensor(acc, acc, s, ALU.mult)
        ve.tensor_scalar(z, V("lru_lambda", 0, DC), 0.0, 8.0, ALU.min, ALU.mult)
        ve.drain()
        ve.scalar_tensor_tensor(out=l8[:, :], in0=acc, scalar=-16.0, in1=z, op0=ALU.mult, op1=ALU.add)
        ve.drain()

    def side(ph, gr, i, j):
        me = j.me
        if gr.kind == "gate":
            ins = ve.drain() if me == "dve" else None
            j.sync("to_act", "dve", "act", ins)
            if me == "act":
                ins = sc.activation(t1[:, :, :], t1[:, :, :], ACT.Gelu_apprx_tanh)
            j.sync("act_to_dve", "act", "dve", ins)
        elif gr.kind in ("q2", "k2"):
            dst, name = (q_2[:, bass.ts(i, 4), :], "q_norm") if gr.kind == "q2" else (k_2[:, :, :], "k_norm")
            n = 4 if gr.kind == "q2" else 2
            head_norm(j, dst, n)
            if me == "dve":
                ve.tensor_scalar(dst, t2[:, 0:n, :], V(name), None, ALU.mult)
                ve.drain()

    @block.sync
    def _(sp):
        sp.dma_start(vec[:, :], vecs).then_inc(consts_in, 16)
        sp.dma_start(res[:, :, :], xT.rearrange("(c p) t -> p c t", p=P)).then_inc(x_in, 16)

        def unit(ph, gr, u, g, n, i):
            if n % 2:
                return
            slot = (u.c // 2) % RAW
            col = gr.col(i)
            if not isinstance(col, int) and n == 0:
                sp.lower_val(col * 4)
            if u.c >= 2 * RAW:
                sp.wait_ge(lo_ready, u.value(1, 2 - 2 * RAW))
            if gr.mode == "GATES":
                src = W[gr.w][:, gr.col(i):gr.col(i) + 48].rearrange("(k p) n -> p k n", p=P)
                dst = wraw[:, slot, 0:DC * 48].rearrange("p (k n) -> p k n", n=48)
                sp.dma_start(dst, src).then_inc(w_loaded[slot], 16)
                return
            k0 = n * UK * P
            rows = W[gr.w][k0:k0 + 4 * P, :].rearrange("(k p) n -> p k n", p=P)
            dst = wraw[:, slot, :].rearrange("p (k n) -> p k n", k=4)
            sp.dma_start(dst[:, :, 0:gr.width], rows[:, :, bass.ds(col, gr.width)]).then_inc(w_loaded[slot], 16)

        walk("sp", sp, unit, nothing)
        sp.wait_ge(residual_done, 1)
        sp.dma_start(outT.rearrange("(c p) t -> p c t", p=P), res[:, :, :]).then_inc(stored, 16)
        sp.wait_ge(stored, 16)

    def split_act(u, act):
        slot, half, r = (u.c // 2) % RAW, u.c % 2, u.c % RING
        act.wait_ge(w_loaded[slot], u.div(2 * RAW).value(16, 16))
        if u.c >= RING:
            act.wait_ge(pe_units, u.value(1, 1 - RING))
        sc.activation(whi[:, r, :], wraw[:, slot, 1024 * half:1024 * half + 1024], ACT.Copy).then_inc(hi_ready, 1)

    EVAC = {"ga": ACT.Sigmoid, "gb": ACT.Sigmoid, "gs": ACT.Sigmoid, "ly": ACT.Gelu_apprx_tanh, "gates": ACT.Sigmoid,
            "ag2": ACT.Silu, "z2": ACT.Silu}

    @block.scalar
    def _(act):
        act.wait_ge(consts_in, 16)
        sc.activation(cs[:, 0, :], V("c", 0, DC), ACT.Silu).then_inc(act_to_dve, 1)
        sc.activation(ltmp[:, 3, :], V("lru_lambda", 0, DC), ACT.Abs)
        sc.drain()
        sc.activation(ltmp[:, 3, :], ltmp[:, 3, :], ACT.Exp, scale=-1.0).then_inc(act_to_dve, 1)
        for n in range(LEAD):
            split_act(Lin(n), act)

        def unit(ph, gr, u, g, n, i):
            if u.terms or u.c + LEAD < N_UNITS:
                split_act(u + LEAD, act)

        def group_end(ph, gr, u, g, i):
            p = g.c % 2
            act.wait_ge(pe_units, u.value())
            if g.c >= 2:
                act.wait_ge(ev_used, g.value(1, -1))
            if gr.mode == "ADA":
                ins = sc.activation(ev[:, p, 0:2, :], pairs[p][:, 0:2, :], ACT.Copy)
            elif gr.mode == "GATES":
                ins = sc.activation(gates[:, :, :], pairs[p][:, 0:4:2, 0:48], ACT.Sigmoid)
            elif gr.kind == "k2":
                ins = sc.activation(ev[:, p, 0:2, :], pairs[p][:, 0:2, :], ACT.Copy)
            elif gr.kind == "v2":
                ins = sc.activation(ev[:, p, 0:4:2, :], pairs[p][:, 0:4:2, :], ACT.Copy)
            elif gr.kind in EVAC:
                ins = sc.activation(ev[:, p, :, :], pairs[p][:, :, :], EVAC[gr.kind])
            elif gr.kind == "gluB":
                for n in range(4):
                    ins = sc.activation(ev[:, p, n, :], pairs[p][:, n, :], ACT.Sigmoid, bias=Vd("b_glu", i * 4 + (8 + n)))
            else:
                ins = sc.activation(ev[:, p, :, :], pairs[p][:, :, :], ACT.Copy)
            ins.then_inc(evacuated, 1)

        walk("act", act, unit, group_end)

    def ada_at(ph, gr, i):
        n = ph.groups.index(gr)
        first, step = {"ada0": (4 * n, 0), "ada1": (8 + 4 * n, 8), "nsa": (32, 4), "lru": (48 + 16 * (n - 2), 4),
                       "nsa3": (44, 0), "out": (80, 4)}[ph.name]
        return i * step + first

    def split_dve(u, dve):
        slot, half, r = (u.c // 2) % RAW, u.c % 2, u.c % RING
        dve.wait_ge(hi_ready, u.value(1, 1))
        ve.tensor_tensor(wlo[:, r, :], wraw[:, slot, 1024 * half:1024 * half + 1024], whi[:, r, :].bitcast(F32),
                         ALU.subtract).then_inc(lo_ready, 1)

    @block.vector
    def _(dve):
        ve.memset(ones[:, :], 1.0).then_inc(to_pool, 1)
        ve.memset(halves[:, :], 0.0)
        ve.drain()
        ve.memset(halves[0:64, 0:64], 1.0)
        ve.memset(halves[64:128, 64:128], 1.0)
        ve.drain()
        dve.wait_ge(act_to_dve, 2)
        ve.tensor_copy(cc[:, :, 0:1].rearrange("p a b -> p (a b)"), cs[:, 0, :])
        ve.drain()
        ve.tensor_tensor(cc[:, :, 1:2].rearrange("p a b -> p (a b)"), cs[:, 0, :],
                         cc[:, :, 0:1].rearrange("p a b -> p (a b)").bitcast(F32), ALU.subtract).then_inc(to_pe, 1)
        dve.wait_ge(x_in, 16)
        dve.wait_ge(consts_in, 16)
        dve.wait_ge(consts_made, 1)
        for n in range(LEAD):
            split_dve(Lin(n), dve)

        def unit(ph, gr, u, g, n, i):
            if u.terms or u.c + LEAD < N_UNITS:
                split_dve(u + LEAD, dve)

        def group_end(ph, gr, u, g, i):
            p = g.c % 2
            e = ev[:, p, :, :]
            dve.wait_ge(evacuated, g.value(1, 1))
            k = gr.kind
            fl = lambda t: t.rearrange("p a b -> p (a b)")
            done = None
            if k == "ada":
                cols = ada_at(ph, gr, i)
                row = ev[:, p, 0:2, :].rearrange("p a (c n) -> p (a c) n", n=P)
                ve.tensor_tensor(row, row, ident[:, :].unsqueeze(1).broadcast_to([P, 4, P]), ALU.mult)
                ve.drain()
                done = ve.tensor_reduce(adat[:, :], row, AX.X, ALU.add)
                ve.drain()
                ve.tensor_tensor(mod[:, bass.ds(cols, 4)], adat[:, :], Vd("ada_b", cols, 4), ALU.add)
            elif k in ("kc", "vc"):
                done = ve.tensor_copy(kc4[:, :, :], e)
            elif k == "k":
                done = ve.tensor_copy(k2[:, bass.ds(i, 1), :, :].rearrange("p o g t -> p (o g) t"), e)
            elif k == "v":
                done = ve.tensor_copy(v2[:, bass.ds(i, 1), :, :].rearrange("p o a b -> p (o a b)"), fl(e))
            elif k == "gates":
                done = ve.drain()
            elif k == "q":
                done = ve.tensor_copy(q4[:, :, :], e)
            elif k == "lx":
                done = conv(t1, e, 4, "lru_conv_w", "lru_conv_b", i * 4, DC)
            elif k == "ly":
                done = ve.tensor_copy(t2[:, :, :], e)
            elif ph.name == "attn_out":
                m = mg2[:, bass.ds(i * 8 + 4 * (ph.groups.index(gr) // 2), 4), :]
                done = ve.tensor_copy(m, e) if k == "ga" else ve.tensor_tensor(m, m, e, ALU.mult)
            elif k in ("ga", "gb"):
                done = ve.tensor_copy(t1[:, :, :], e)
            elif k == "pa":
                done = ve.tensor_tensor(res[:, bass.ts(i, 4), :], t1[:, :, :], e, ALU.mult)
            elif k == "pb":
                m = res
                done = ve.tensor_tensor(t2[:, :, :], t1[:, :, :], e, ALU.mult)
                ve.drain()
                ve.tensor_tensor(m[:, bass.ts(i, 4), :], m[:, bass.ts(i, 4), :], t2[:, :, :], ALU.add)
            elif k in ("wout", "down"):
                g0 = 32 if k == "wout" else 80
                for n in range(4):
                    c = i * 4 + n if k == "wout" else i * 8 + (4 * ph.groups.index(gr) + n)
                    done = ve.scalar_tensor_tensor(out=res[:, bass.ds(c, 1), :].rearrange("p o t -> p (o t)"),
                                                   in0=e[:, n, :], scalar=mod[:, bass.ds(c + g0, 1)],
                                                   in1=res[:, bass.ds(c, 1), :].rearrange("p o t -> p (o t)"),
                                                   op0=ALU.mult, op1=ALU.add)
            elif k == "wout2":
                c = gr.col(0) // P
                done = ve.tensor_tensor(res[:, c:c + 4, :], res[:, c:c + 4, :], e, ALU.add)
            elif k == "gate":
                first = 24 if ph.name == "up1" else 0
                done = conv(t1, e, 3, "ffn_conv_w", "ffn_conv_b", i * 4 + first, FFC)
            elif k == "val":
                done = ve.tensor_tensor(t2[:, :, :], t1[:, :, :], e, ALU.mult)
                ve.drain()
                split(hid, i * 4, 4, t2[:, :, :])
            elif k == "u2":
                done = ve.tensor_copy(u_2[:, bass.ts(i, 4), :], e)
            elif k == "q2":
                done = ve.tensor_copy(q_2[:, bass.ts(i, 4), :], e)
            elif k == "k2":
                done = ve.tensor_copy(k_2[:, :, :], ev[:, p, 0:2, :])
            elif k == "v2":
                done = ve.tensor_copy(v_2[:, :, :], ev[:, p, 0:4:2, :])
            elif k == "ag2":
                done = ve.tensor_copy(ag_2[:, bass.ts(i, 4), :], e)
            elif k == "z2":
                done = ve.tensor_copy(z_2[:, bass.ts(i, 4), :], e)
            elif k == "gs":
                done = ve.tensor_copy(gs_2[:, bass.ds(i * 8 + 4 * ph.groups.index(gr), 4), :], e)
            elif k == "ps":
                c = i * 8 + 4 * ph.groups.index(gr)
                done = ve.tensor_tensor(t2[:, :, :], gs_2[:, bass.ds(c, 4), :], e, ALU.mult)
                ve.drain()
                ve.tensor_tensor(mg2[:, bass.ds(c, 4), :], mg2[:, bass.ds(c, 4), :], t2[:, :, :], ALU.add)
            elif k == "gluA":
                for n in range(4):
                    done = ve.scalar_tensor_tensor(out=t1[:, n, :], in0=e[:, n, :], scalar=Vd("b_glu", i * 4 + n),
                                                   in1=z_2[:, bass.ds(i * 4 + n, 1), :].rearrange("p o t -> p (o t)"),
                                                   op0=ALU.add, op1=ALU.mult)
            elif k == "gluB":
                done = ve.tensor_tensor(t2[:, :, :], t1[:, :, :], e, ALU.mult)
                ve.drain()
                split(sg, i * 4, 4, t2[:, :, :])
            done.then_inc(ev_used, 1)
            ve.drain()

        walk("dve", dve, unit, group_end)
        ve.drain().then_inc(residual_done, 1)

    @block.tensor
    def _(pe):
        pe.wait_ge(to_pe, 1)
        pe.wait_ge(consts_made, 1)

        def unit(ph, gr, u, g, n, i):
            r = u.c % RING
            pair = pairs[g.c % 2]
            if n == 0 and g.c >= 2:
                pe.wait_ge(evacuated, g.value(1, -1))
            pe.wait_ge(lo_ready, u.value(1, 1))
            K = 2 * UK * gr.slots
            if gr.mode == "ADA":
                for kk in range(UK):
                    k = n * UK + kk
                    for t, (w, part) in enumerate(((whi, 0), (whi, 1), (wlo, 0))):
                        ins = te.matmul(pair[:, 0:2, :].rearrange("p a b -> p (a b)"),
                                        cc[:, k, part:part + 1].broadcast_to([P, P]), w[:, r, kk * CB:(kk + 1) * CB],
                                        start=(k == 0 and t == 0), stop=(k == K - 1 and t == 2))
            elif gr.mode == "T":
                whv = whi[:, r, :].rearrange("p (k n) -> p k n", k=UK)
                wlv = wlo[:, r, :].rearrange("p (k n) -> p k n", k=UK)
                hi, lo = X[gr.x]
                for kk in range(UK):
                    k = n * UK + kk
                    for o in range(gr.width // P):
                        for t, (w, x) in enumerate(((whv, hi), (whv, lo), (wlv, hi))):
                            ins = te.matmul(pair[:, o, :], w[:, kk, o * P:(o + 1) * P], x[:, k, :],
                                            start=(k == 0 and o % 2 == 0 and t == 0),
                                            stop=(k == K - 1 and t == 2), skip_group_check=True)
            else:
                hi, lo = X[gr.x]
                if gr.mode == "GATES":
                    ks, wd = DC * (n == 0), 48
                    ins = pe.drain() if n else None
                else:
                    ks, wd = UK, gr.width
                for kk in range(ks):
                    k = n * ks + kk
                    if gr.mode == "GATES":
                        view = lambda w: w[:, r, kk * 48:(kk + 1) * 48]
                    else:
                        view = lambda w: w[:, r, kk * 512:kk * 512 + wd]
                    for b in range(2):
                        for t, (w, x) in enumerate(((whi, hi), (whi, lo), (wlo, hi))):
                            dst = pair[:, 2 * b:2 * b + 2, :].rearrange("p a b -> p (a b)")[:, 0:wd]
                            ins = te.matmul(dst, x[:, k, b * P:(b + 1) * P], view(w), start=(k == 0 and t == 0),
                                            stop=(k == 15 and t == 2))
            ins.then_inc(pe_units, 1)

        walk("pe", pe, unit, nothing)

    @block.gpsimd
    def _(pool):
        pool.wait_ge(to_pool, 1)
        po.memset(causal[:, :, :], 0.0)
        po.memset(band[:, :], 0.0)
        po.memset(cmask[:, :, :], 1.0)
        po.memset(cadd[:, :, :], 0.0)
        po.drain()
        po.affine_select(out=causal[:, :, :], in_=causal[:, :, :], compare_op=ALU.is_ge, fill=NEG, base=0,
                         pattern=[[P, 2], [-1, T]], channel_multiplier=1)
        po.affine_select(out=band[:, :], in_=band[:, :], compare_op=ALU.is_ge, fill=NEG, base=-1,
                         pattern=[[1, T]], channel_multiplier=-1)
        po.affine_select(out=cmask[:, :, :], in_=cmask[:, :, :], compare_op=ALU.is_ge, fill=0.0, base=-31,
                         pattern=[[P, 2], [-16, 16]], channel_multiplier=1)
        po.affine_select(out=cadd[:, :, :], in_=cadd[:, :, :], compare_op=ALU.is_ge, fill=NEG, base=-31,
                         pattern=[[P, 2], [-16, 16]], channel_multiplier=1)
        po.affine_select(out=ident[:, :], in_=ones[:, :], compare_op=ALU.is_equal, fill=0.0, base=0,
                         pattern=[[-1, P]], channel_multiplier=1)
        po.drain()
        po.affine_select(out=band[:, :], in_=band[:, :], compare_op=ALU.is_ge, fill=NEG, base=P,
                         pattern=[[-1, T]], channel_multiplier=1)
        po.drain()
        po.drain().then_inc(consts_made, 1)
        walk("pool", pool, nothing, nothing)



def kernel(**inputs):
    import numpy as np
    import concourse.bacc as bacc
    from concourse.bass_utils import run_bass_kernel_spmd as run

    nc = bacc.Bacc("TRN2", target_bir_lowering=False, num_devices=1)
    arrays = {}

    def dram(name, a):
        a = np.ascontiguousarray(a)
        arrays[name + "_dram"] = a
        return nc.dram_tensor(name + "_dram", a.shape, F32, kind="ExternalInput").ap()

    v = {k: np.asarray(a) for k, a in inputs.items()}
    cols = lambda a: a.reshape(-1, P).T
    packed = {
        "c": cols(v["c"]), "ada_b": cols(v["ada_b"]), "norm1_g": cols(v["norm1_g"]), "norm2_g": cols(v["norm2_g"]),
        "final_g": cols(v["final_g"]), "norm_w_2": cols(v["norm_w_2"]), "lru_conv_w": cols(v["lru_conv_w"]),
        "lru_conv_b": cols(v["lru_conv_b"]), "lru_ba": cols(v["lru_ba"]), "lru_bi": cols(v["lru_bi"]),
        "lru_lambda": cols(v["lru_lambda"]), "ffn_conv_w": cols(v["ffn_conv_w"]), "ffn_conv_b": cols(v["ffn_conv_b"]),
        "cmp_pos_k": v["cmp_pos_k"][0].T, "cmp_pos_v": v["cmp_pos_v"][0].T,
        "q_norm": np.concatenate([v["q_norm_w_2"]] * 2)[:, None], "k_norm": np.concatenate([v["k_norm_w_2"]] * 2)[:, None],
        "sinks": np.broadcast_to(v["sinks_2"], (P, 16)), "A_re": cols(v["A_re_2"]), "A_im": cols(v["A_im_2"]),
        "log_dt": cols(np.repeat(v["log_dt_2"], 64)), "D_skip": cols(v["D_skip_2"]), "b_glu": cols(v["b_glu_2"]),
    }
    vecs = dram("vecs", np.concatenate([packed[name] for name, _ in VEC_SIZES], axis=1))
    xT = dram("xT", v["x"][0].T)
    W = {name: dram(name, v[name][0]) for name in ("ada_w", "w_in", "proj_a", "proj_b", "w_out", "ffn_up", "ffn_down")}
    W.update({name: dram(name, v[name]) for name in ("w_in_2", "w_attn_proj_2", "w_glu_2", "w_ssm_proj_2", "w_out_2")})
    W["ffn_down0"], W["ffn_down1"] = W["ffn_down"][0:FF // 2, :], W["ffn_down"][FF // 2:FF, :]
    B = np.zeros((9, 4, 2, 16, 2, 2, 64), np.float32)
    C = np.zeros((9, 2, 64, 2, 4, 2, 16), np.float32)
    for part, (b, c) in enumerate((("B_re_2", "C_re_2"), ("B_im_2", "C_im_2"))):
        b = v[b].reshape(8, 4, 2, 64, 16)
        c = v[c].reshape(8, 4, 2, 16, 64)
        for e in range(2):
            B[:8, :, e, :, part, e, :] = b[:, :, e].transpose(0, 1, 3, 2)
            C[:8, e, :, part, :, e, :] = c[:, :, e].transpose(0, 3, 1, 2)
    small = {
        "cmp_w1": [dram("cmp_w1_k", v["cmp_w1_k"][0]), dram("cmp_w1_v", v["cmp_w1_v"][0])],
        "cmp_w2": [dram("cmp_w2_k", v["cmp_w2_k"][0]), dram("cmp_w2_v", v["cmp_w2_v"][0])],
        "lru_wa": dram("lru_wa", v["lru_wa"][0]), "lru_wi": dram("lru_wi", v["lru_wi"][0]),
        "B": dram("B", B.reshape(9, P, 2, P)), "C": dram("C", C.reshape(9, P, 2, 4, 32)),
    }
    outT = nc.dram_tensor("outT_dram", (D, T), F32, kind="ExternalOutput").ap()
    with ExitStack() as ctx:
        build_program(nc, ctx, xT, vecs, W, small, outT)
    r = run(nc, [arrays], core_ids=[0])
    return np.ascontiguousarray(r.results[0]["outT_dram"].T)[None]
```
